# Optimizing a Trainium2 kernel written in Bass

```python
import jax, jax.numpy as jnp
from jax import lax
import numpy as np

D_MODEL = 1024
BATCH = 1
SEQ = 512
DEPTH = 1

HEAD_DIM = 64
N_HEADS_SB = 8
N_HEADS_FOX = 8
D_SB = N_HEADS_SB * HEAD_DIM
D_FOX = N_HEADS_FOX * HEAD_DIM
D_FF = 2816
CONV_WIDTH = 3
Q_BLOCK = 128
LN_EPS = 1e-5
DEEPNORM_ALPHA = (2.0 * DEPTH) ** 0.25
DEEPNORM_BETA = (8.0 * DEPTH) ** -0.25
FORGET_BIAS_MEAN = 3.0

SPLIT_SIZES = (D_SB, D_SB, D_SB, D_FOX, D_FOX, D_FOX, N_HEADS_FOX, D_MODEL, D_MODEL)
SPLIT_POINTS = tuple(int(v) for v in np.cumsum(SPLIT_SIZES)[:-1])
N_IN = int(sum(SPLIT_SIZES))

kernel_name = 'hybrid_stickbreak_fox_convglu_deepnorm'

def layer_norm(x, g, b):
    xf = x.astype(jnp.float32)
    mean = jnp.mean(xf, axis=-1, keepdims=True)
    var = jnp.mean(jnp.square(xf - mean), axis=-1, keepdims=True)
    y = (xf - mean) * lax.rsqrt(var + LN_EPS)
    return (y * g.astype(jnp.float32) + b.astype(jnp.float32)).astype(x.dtype)

def split_heads(t, n_heads):
    b, s, _ = t.shape
    return t.reshape(b, s, n_heads, HEAD_DIM).transpose(0, 2, 1, 3)

def merge_heads(t):
    b, h, s, d = t.shape
    return t.transpose(0, 2, 1, 3).reshape(b, s, h * d)

def stick_breaking_attention(q, k, v):
    seq = q.shape[2]
    scale = HEAD_DIM ** -0.5
    outs = []
    for i in range(seq // Q_BLOCK):
        end = (i + 1) * Q_BLOCK
        qb = q[:, :, i * Q_BLOCK:end]
        kb, vb = k[:, :, :end], v[:, :, :end]
        z = jnp.einsum('bhqd,bhkd->bhqk', qb, kb).astype(jnp.float32) * scale
        q_pos = jnp.arange(i * Q_BLOCK, end)
        k_pos = jnp.arange(end)
        strict = k_pos[None, :] < q_pos[:, None]
        log_beta = jax.nn.log_sigmoid(z)
        log_one_minus = jnp.where(strict, jax.nn.log_sigmoid(-z), 0.0)
        suffix = lax.cumsum(log_one_minus, axis=3, reverse=True) - log_one_minus
        weights = jnp.where(strict, jnp.exp(log_beta + suffix), 0.0)
        outs.append(jnp.einsum('bhqk,bhkd->bhqd', weights.astype(vb.dtype), vb))
    return jnp.concatenate(outs, axis=2)

def forgetting_attention(q, k, v, cum_log_f):
    seq = q.shape[2]
    scale = HEAD_DIM ** -0.5
    outs = []
    for i in range(seq // Q_BLOCK):
        end = (i + 1) * Q_BLOCK
        qb = q[:, :, i * Q_BLOCK:end]
        kb, vb = k[:, :, :end], v[:, :, :end]
        c_q = cum_log_f[:, :, i * Q_BLOCK:end]
        c_k = cum_log_f[:, :, :end]
        z = jnp.einsum('bhqd,bhkd->bhqk', qb, kb).astype(jnp.float32) * scale
        z = z + c_q[..., :, None] - c_k[..., None, :]
        q_pos = jnp.arange(i * Q_BLOCK, end)
        k_pos = jnp.arange(end)
        causal = k_pos[None, :] <= q_pos[:, None]
        p = jax.nn.softmax(jnp.where(causal, z, -jnp.inf), axis=-1)
        outs.append(jnp.einsum('bhqk,bhkd->bhqd', p.astype(vb.dtype), vb))
    return jnp.concatenate(outs, axis=2)

def causal_depthwise_conv(u, w_conv, b_conv):
    seq = u.shape[1]
    u_pad = jnp.pad(u, ((0, 0), (CONV_WIDTH - 1, 0), (0, 0)))
    y = b_conv
    for tap in range(CONV_WIDTH):
        y = y + w_conv[tap] * u_pad[:, tap:tap + seq]
    return y

def setup_inputs(seed: int = 0) -> dict:
    key = jax.random.key(seed)
    ks = jax.random.split(key, 16)
    f32 = jnp.float32
    x = jax.random.normal(ks[0], (BATCH, SEQ, D_MODEL), f32)
    col_scale = np.ones((N_IN,), np.float32)
    bounds = (0,) + SPLIT_POINTS + (N_IN,)
    for idx in (2, 5):
        col_scale[bounds[idx]:bounds[idx + 1]] = DEEPNORM_BETA
    bias_offset = np.zeros((N_IN,), np.float32)
    bias_offset[bounds[6]:bounds[7]] = FORGET_BIAS_MEAN
    w_in = jax.random.normal(ks[1], (DEPTH, D_MODEL, N_IN), f32) * D_MODEL ** -0.5 * jnp.asarray(col_scale)
    b_in = 0.02 * jax.random.normal(ks[2], (DEPTH, N_IN), f32) + jnp.asarray(bias_offset)
    w_proj_sb = jax.random.normal(ks[3], (DEPTH, D_SB, D_MODEL), f32) * D_SB ** -0.5 * DEEPNORM_BETA
    w_proj_fox = jax.random.normal(ks[4], (DEPTH, D_FOX, D_MODEL), f32) * D_FOX ** -0.5 * DEEPNORM_BETA
    w_out = jax.random.normal(ks[5], (DEPTH, D_MODEL, D_MODEL), f32) * D_MODEL ** -0.5 * DEEPNORM_BETA
    ln1_g = 1.0 + 0.02 * jax.random.normal(ks[6], (DEPTH, D_MODEL), f32)
    ln1_b = 0.02 * jax.random.normal(ks[7], (DEPTH, D_MODEL), f32)
    w_up = jax.random.normal(ks[8], (DEPTH, D_MODEL, 2 * D_FF), f32) * D_MODEL ** -0.5
    w_conv = jax.random.normal(ks[9], (DEPTH, CONV_WIDTH, D_FF), f32) * CONV_WIDTH ** -0.5
    b_conv = 0.02 * jax.random.normal(ks[10], (DEPTH, D_FF), f32)
    w_down = jax.random.normal(ks[11], (DEPTH, D_FF, D_MODEL), f32) * D_FF ** -0.5 * DEEPNORM_BETA
    ln2_g = 1.0 + 0.02 * jax.random.normal(ks[12], (DEPTH, D_MODEL), f32)
    ln2_b = 0.02 * jax.random.normal(ks[13], (DEPTH, D_MODEL), f32)
    return {'x': x, 'w_in': w_in, 'b_in': b_in, 'w_proj_sb': w_proj_sb,
            'w_proj_fox': w_proj_fox, 'w_out': w_out, 'ln1_g': ln1_g, 'ln1_b': ln1_b,
            'w_up': w_up, 'w_conv': w_conv, 'b_conv': b_conv, 'w_down': w_down,
            'ln2_g': ln2_g, 'ln2_b': ln2_b}

def reference(x, w_in, b_in, w_proj_sb, w_proj_fox, w_out, ln1_g, ln1_b,
              w_up, w_conv, b_conv, w_down, ln2_g, ln2_b):
    for l in range(DEPTH):
        h = jnp.einsum('bsd,dn->bsn', x, w_in[l]) + b_in[l]
        q_sb, k_sb, v_sb, q_fx, k_fx, v_fx, f_logit, g_sb, g_fx = jnp.split(h, SPLIT_POINTS, axis=-1)
        o_sb = stick_breaking_attention(split_heads(q_sb, N_HEADS_SB),
                                        split_heads(k_sb, N_HEADS_SB),
                                        split_heads(v_sb, N_HEADS_SB))
        cum_log_f = lax.cumsum(jax.nn.log_sigmoid(f_logit.astype(jnp.float32)), axis=1)
        o_fx = forgetting_attention(split_heads(q_fx, N_HEADS_FOX),
                                    split_heads(k_fx, N_HEADS_FOX),
                                    split_heads(v_fx, N_HEADS_FOX),
                                    cum_log_f.transpose(0, 2, 1))
        y_sb = jnp.einsum('bse,ed->bsd', merge_heads(o_sb), w_proj_sb[l])
        y_fx = jnp.einsum('bse,ed->bsd', merge_heads(o_fx), w_proj_fox[l])
        merged = jax.nn.sigmoid(g_sb) * y_sb + jax.nn.sigmoid(g_fx) * y_fx
        mix = jnp.einsum('bsd,de->bse', merged, w_out[l])
        x = layer_norm(DEEPNORM_ALPHA * x + mix, ln1_g[l], ln1_b[l])
        u = jnp.einsum('bsd,df->bsf', x, w_up[l])
        u_gate, u_val = jnp.split(u, 2, axis=-1)
        a = jax.nn.gelu(causal_depthwise_conv(u_gate, w_conv[l], b_conv[l]), approximate=False) * u_val
        ffn = jnp.einsum('bsf,fd->bsd', a, w_down[l])
        x = layer_norm(DEEPNORM_ALPHA * x + ffn, ln2_g[l], ln2_b[l])
    return x


_drawn_inputs = setup_inputs


def setup_inputs(seed=0):
    import zlib

    import numpy as np

    out = dict(_drawn_inputs(seed))
    spreads = {}
    factors = {'ln1_b': 2.741, 'b_conv': 8.0, 'ln2_g': 2.892, 'ln2_b': 2.747}
    for name, (base, spread) in spreads.items():
        noise = np.random.default_rng([zlib.crc32(name.encode()), seed]).standard_normal(out[name].shape)
        drawn = base * np.exp(spread * noise) if base else spread * noise
        out[name] = __import__('jax').numpy.asarray(drawn.astype(out[name].dtype))
    for name, factor in factors.items():
        out[name] = (out[name] * factor).astype(out[name].dtype)
    return out
```

```python
import concourse.bass as bass
from concourse import mybir
from contextlib import ExitStack

P = 128
D_MODEL = 1024
SEQ = 512
HEAD_DIM = 64
D_SB = 512
D_FOX = 512
N_FORGET = 8
D_FF = 2816
CONV_WIDTH = 3
LN_EPS = 1e-5
ALPHA = 2.0 ** 0.25

KB = D_MODEL // P
SB = SEQ // P
FB = D_FF // P
PAIRS = D_SB // P
HALVES = 2 * PAIRS
NG = 2 * KB
BIG = 1e30

N_F = KB
N_QK0 = N_F + 1
N_PAIR = N_QK0 + 4
N_LAST = N_PAIR + 8 * (PAIRS - 1)
N_MERGE = N_LAST + 4
N_UP = N_MERGE + 2 * KB
N_DOWN = N_UP + 2 * FB
N_BLOCKS = N_DOWN + FB
W_SLOTS = 4
RESIDENT = 4

COL_QK = 0
COL_G = COL_QK + 4 * PAIRS
COL_F = COL_G + NG
COL_CW = COL_F + 1
COL_CB = COL_CW + CONV_WIDTH * FB
COL_SEL = COL_CB + FB
COL_MASK = COL_SEL + 6
N_COLS = COL_MASK + N_FORGET

SB_OFF = [0, 512, 1024, 896]
FX_OFF = [896, 1024, 512, 0]
FLAT = 1280


def layer(nc, xT, x_tok, w_stream, cols, rows, square, out):
    f32, f32r, bf16 = mybir.dt.float32, mybir.dt.float32r, mybir.dt.bfloat16
    ACT, ALU, AX = mybir.ActivationFunctionType, mybir.AluOpType, mybir.AxisListType
    ds = bass.ds

    K = 1024
    area_w = (nc.sbuf_base + 63) // 64 * 64
    area_x, area_o, area_g = area_w + 32 * K, area_w + 64 * K, area_w + 96 * K
    area_a, area_c = area_w + 128 * K, area_w + 196 * K
    assert area_c + 6 * K <= nc.sbuf_usable_end

    def at(name, shape, dt, offset):
        return nc.alloc_sbuf_tensor_at(name, shape, dt, offset=offset)

    w_raw = at("w_raw", [P, W_SLOTS, 1024], f32, area_w)
    w_lo = at("w_lo", [P, W_SLOTS, 1024], f32r, area_w)
    w_hi = at("w_hi", [P, W_SLOTS, 1024], f32r, area_w + 16 * K)
    xT_hi = at("xT_hi", [P, KB, SEQ], f32r, area_x)
    xT_lo = at("xT_lo", [P, KB, SEQ], f32r, area_x + 16 * K)
    mT_hi = at("mT_hi", [P, KB, SEQ], f32r, area_x)
    mT_lo = at("mT_lo", [P, KB, SEQ], f32r, area_x + 16 * K)
    a_hi = at("a_hi", [P, W_SLOTS, SEQ], f32r, area_x)
    a_lo = at("a_lo", [P, W_SLOTS, SEQ], f32r, area_x + 8 * K)
    oT_hi = at("oT_hi", [P, KB, SEQ], f32r, area_o)
    oT_lo = at("oT_lo", [P, KB, SEQ], f32r, area_o + 16 * K)
    x1T_hi = at("x1T_hi", [P, KB, SEQ], f32r, area_o)
    x1T_lo = at("x1T_lo", [P, KB, SEQ], f32r, area_o + 16 * K)
    xT_raw = at("xT_raw", [P, KB, SEQ], f32, area_g)
    f_e = at("f_e", [P, SEQ], f32, area_g + 16 * K)
    f_min = at("f_min", [P, SEQ], f32, area_g + 18 * K)
    f_log = at("f_log", [P, SEQ], f32, area_g + 20 * K)
    f_zero = at("f_zero", [P, SEQ], f32, area_g + 22 * K)
    f_cum = at("f_cum", [P, SEQ], f32, area_g + 24 * K)
    f_hi = at("f_hi", [P, SEQ], f32r, area_g + 26 * K)
    f_lo = at("f_lo", [P, SEQ], f32r, area_g + 28 * K)
    f_tmp = at("f_tmp", [P, SEQ], f32, area_g + 30 * K)
    g_all = at("g_all", [P, NG, SEQ], f32, area_g)
    x1 = at("x1", [P, SB, D_MODEL], f32, area_g)
    ln_rows = at("ln_rows", [P, 4, D_MODEL], f32, area_g + 16 * K)
    v_all = at("v_all", [P, SB, 1024], f32, area_a)
    qk_hi = at("qk_hi", [P, 4, SEQ], f32r, area_a + 16 * K)
    qk_lo = at("qk_lo", [P, 4, SEQ], f32r, area_a + 24 * K)
    qk_t = at("qk_t", [P, 2, SEQ], f32, area_a + 32 * K)
    v_hi = at("v_hi", [P, 2, SB, P], f32r, area_a + 36 * K)
    v_lo = at("v_lo", [P, 2, SB, P], f32r, area_a + 40 * K)
    sb_t = at("sb_t", [P, FLAT], f32, area_a + 44 * K)
    sb_lo = at("sb_lo", [P, FLAT], f32r, area_a + 44 * K)
    sb_hi = at("sb_hi", [P, FLAT], f32r, area_a + 49 * K)
    fx_p = at("fx_p", [P, FLAT], f32, area_a + 54 * K)
    fx_hi = at("fx_hi", [P, FLAT], f32r, area_a + 54 * K)
    fx_lo = at("fx_lo", [P, FLAT], f32r, area_a + 59 * K)
    f_rhs = at("f_rhs", [P, SEQ], f32r, area_a + 64 * K)
    f_sel = at("f_sel", [P, SEQ], f32r, area_a + 66 * K)
    vb_row = at("vb_row", [P, 1024], f32, area_a + 44 * K)
    sq_raw = at("sq_raw", [P, 5, P], f32, area_a + 54 * K)
    wout_hi = at("wout_hi", [P, KB, D_MODEL], f32r, area_a)
    wout_lo = at("wout_lo", [P, KB, D_MODEL], f32r, area_a + 32 * K)
    mg_t = at("mg_t", [P, 2, SEQ], f32, area_a + 64 * K)
    aT = at("aT", [P, FB, SEQ], f32, area_a)
    conv = at("conv", [P, 2, SEQ], f32, area_a + 44 * K)
    gelu = at("gelu", [P, 2, SEQ], f32, area_a + 48 * K)
    f_lhs = at("f_lhs", [P, SEQ], f32, area_c)
    col = at("col", [P, N_COLS], f32, area_c + 2048)
    ident = at("ident", [P, P], f32, area_c + 2048 + 576)
    neg_tri = at("neg_tri", [P, P], f32r, area_c + 2624 + 512)
    neg_one = at("neg_one", [P, P], f32r, area_c + 2624 + 1024)
    ident_bf = at("ident_bf", [P, P], bf16, area_c + 2624 + 1536)
    mask_bf = at("mask_bf", [P, 2, P], bf16, area_c + 2624 + 1792)
    small = area_c + 2624 + 2304
    q_bias = at("q_bias", [P, 4 * PAIRS], f32, small)
    fx_nmax = at("fx_nmax", [P, SB], f32, small + 64)
    fx_sum = at("fx_sum", [P, SB], f32, small + 96)
    fx_rec = at("fx_rec", [P, SB], f32, small + 128)
    bn_parts = at("bn_parts", [P, 2, 6], f32, small + 160)
    bn_mv = at("bn_mv", [P, 2], f32, small + 224)
    ln_var = at("ln_var", [P, 1], f32, small + 256)
    ln_log = at("ln_log", [P, 1], f32, small + 288)
    ln_r0 = at("ln_r0", [P, 1], f32, small + 320)
    ln_nt = at("ln_nt", [P, 1], f32, small + 352)
    ln_r = at("ln_r", [P, 1], f32, small + 384)
    assert COL_MASK + N_FORGET == N_COLS and 4 * N_COLS <= 576

    def plain(ap):
        return ap.bitcast(f32)

    with ExitStack() as ctx:
        ps = ctx.enter_context(nc.psum_tensor("ps", [P, 8 * 512], f32))

        def bank(i):
            return ps[:, 512 * i:512 * (i + 1)]

        SB_PS, FX_PS = 0, 3 * 512

        def sem(name):
            return ctx.enter_context(nc.semaphore(name))

        raw_in = [sem(f"raw_in{i}") for i in range(W_SLOTS)]
        x_in = [sem(f"x_in{k}") for k in range(KB)]
        const_in, vb_in, row_in = sem("const_in"), sem("vb_in"), sem("row_in")
        tok_in = [sem(f"tok_in{s}") for s in range(SB)]
        stored = sem("stored")
        hi_ready, lo_ready = sem("hi_ready"), sem("lo_ready")
        block_done = sem("block_done")
        xhi_ready, xlo_ready = sem("xhi_ready"), sem("xlo_ready")
        const_ready = sem("const_ready")
        v_ready = sem("v_ready")
        f_absed, f_exped, f_lned = sem("f_absed"), sem("f_exped"), sem("f_lned")
        f_mined, f_logged, f_cumed = sem("f_mined"), sem("f_logged"), sem("f_cumed")
        f_split, f_lo_done, f_part, f_ready = sem("f_split"), sem("f_lo_done"), sem("f_part"), sem("f_ready")
        block_read = sem("block_read")
        qk_biased, qk_hi_done, qk_split = sem("qk_biased"), sem("qk_hi_done"), sem("qk_split")
        v_hi_done, v_split = sem("v_hi_done"), sem("v_split")
        sel_ready = sem("sel_ready")
        sb_scored, sb_summed, sb_mixed = sem("sb_scored"), sem("sb_summed"), sem("sb_mixed")
        sb_absed, sb_exped, sb_lned, sb_weighed = (sem("sb_absed"), sem("sb_exped"), sem("sb_lned"),
                                                   sem("sb_weighed"))
        sb_soft, sb_soft_hi, sb_soft_split = sem("sb_soft"), sem("sb_soft_hi"), sem("sb_soft_split")
        sb_w_hi, sb_w_split = sem("sb_w_hi"), sem("sb_w_split")
        fx_scored, fx_turned, fx_mixed = sem("fx_scored"), sem("fx_turned"), sem("fx_mixed")
        fx_maxed, fx_exped, fx_inverted, fx_normed = (sem("fx_maxed"), sem("fx_exped"), sem("fx_inverted"),
                                                      sem("fx_normed"))
        fx_w_hi, fx_w_split = sem("fx_w_hi"), sem("fx_w_split")
        o_hi_done, o_split = [sem("sb_o_hi"), sem("fx_o_hi")], [sem("sb_o_split"), sem("fx_o_split")]
        gated = sem("gated")
        mg_a, mg_b, mg_sum, mg_hi, merged = sem("mg_a"), sem("mg_b"), sem("mg_sum"), sem("mg_hi"), sem("merged")
        out_done = sem("out_done")
        ln_added, ln_stated, ln_aggred, ln_vared = sem("ln_added"), sem("ln_stated"), sem("ln_aggred"), sem("ln_vared")
        ln_logged, ln_rooted, ln_newton, ln_halved, ln_scale = (sem("ln_logged"), sem("ln_rooted"), sem("ln_newton"),
                                                                sem("ln_halved"), sem("ln_scale"))
        ln_normed, ln_gained, ln_done = sem("ln_normed"), sem("ln_gained"), sem("ln_done")
        x1_turned, x1_hi_done, x1_split = sem("x1_turned"), sem("x1_hi_done"), sem("x1_split")
        cv_biased, cv_one, cv_done, gelu_done = sem("cv_biased"), sem("cv_one"), sem("cv_done"), sem("gelu_done")
        act_ready, a_hi_done, a_split = sem("act_ready"), sem("a_hi_done"), sem("a_split")

        USED_PAIRS = N_MERGE
        USED_MERGE = USED_PAIRS + KB
        USED_UP = USED_MERGE + 2 * FB
        UP_LAG = N_UP - USED_MERGE
        FREE = 1
        FREE_MERGE = 4
        FREE_ACT = 2

        block = ctx.enter_context(nc.Block())

        @block.sync
        def _(sp):
            def load(n, slot):
                sp.dma_start(w_raw[:, slot, :], w_stream[ds(n, 1), :, :].rearrange("o p c -> p (o c)")
                             if not isinstance(n, int) else w_stream[n, :, :]).then_inc(raw_in[slot], 16)

            def load_x(k):
                sp.dma_start(xT_raw[:, k, :], xT[k, :, :]).then_inc(x_in[k], 16)

            for k in range(W_SLOTS):
                load_x(k)
                load(k, k)
            for k in range(W_SLOTS, KB):
                load_x(k)
            sp.dma_start(col[:], cols).then_inc(const_in, 16)
            sp.dma_start(ident[:], square[:, 0, :]).then_inc(const_in, 16)
            sp.dma_start(sq_raw[:], square).then_inc(const_in, 16)
            sp.dma_start(vb_row[:], rows[0, :].partition_broadcast(P)).then_inc(vb_in, 16)
            with sp.Fori(0, (N_LAST + 3 - W_SLOTS) // 4) as i:
                for j in range(4):
                    sp.wait_ge(block_done, 4 * i + (j + 1))
                    load(4 * i + (4 + j), j)
            for n in range(N_LAST + 3, N_MERGE + 3):
                sp.wait_ge(block_done, n - 3)
                load(n, n % 4)
            sp.wait_ge(block_done, N_MERGE)
            load(N_MERGE + 3, (N_MERGE + 3) % 4)
            with sp.Fori(0, 3) as i:
                for j in range(2):
                    sp.wait_ge(block_done, 2 * i + (USED_PAIRS + 1 + j))
                    load(4 * i + (N_MERGE + 4 + 2 * j), (N_MERGE + 2 * j) % 4)
                    sp.wait_ge(lo_ready, 4 * i + (N_MERGE + 2 + 2 * j))
                    load(4 * i + (N_MERGE + 5 + 2 * j), (N_MERGE + 1 + 2 * j) % 4)
            for j in range(2):
                sp.wait_ge(block_done, USED_MERGE - 1 + j)
                load(N_UP + 2 * j, (N_UP + 2 * j) % 4)
                sp.wait_ge(lo_ready, N_UP - 2 + 2 * j)
                load(N_UP + 1 + 2 * j, (N_UP + 1 + 2 * j) % 4)
            sp.wait_ge(merged, KB + FREE_MERGE)
            for s in range(SB):
                sp.dma_start(x1[:, s, :], x_tok[P * s:P * (s + 1), :]).then_inc(tok_in[s], 16)
                if s == 0:
                    for r in range(4):
                        sp.dma_start(ln_rows[:, r, :], rows[1 + r, :].partition_broadcast(P)).then_inc(row_in, 16)
            with sp.Fori(0, (N_BLOCKS - N_UP - 4) // 4) as i:
                for j in range(4):
                    sp.wait_ge(block_done, 4 * i + (USED_MERGE + 1 + j))
                    load(4 * i + (N_UP + 4 + j), (N_UP + j) % 4)
            for n in range(N_UP + 4 + (N_BLOCKS - N_UP - 4) // 4 * 4, N_BLOCKS):
                sp.wait_ge(block_done, n - W_SLOTS - UP_LAG + 1)
                load(n, n % 4)
            for s in range(SB):
                sp.wait_ge(ln_done, SB + s + 1)
                sp.dma_start(out[P * s:P * (s + 1), :], x1[:, s, :]).then_inc(stored, 16)
            sp.wait_ge(stored, 16 * SB)

        @block.gpsimd
        def _(pool):
            def low(n, slot):
                pool.wait_ge(hi_ready, n + 1)
                nc.gpsimd.tensor_tensor(w_lo[:, slot, :], w_raw[:, slot, :], plain(w_hi[:, slot, :]),
                                        ALU.subtract).then_inc(lo_ready, 1)

            def low_out(n, slot, k):
                pool.wait_ge(hi_ready, n + 1)
                nc.gpsimd.tensor_tensor(wout_lo[:, ds(k, 1), :].rearrange("p o c -> p (o c)"), w_raw[:, slot, :],
                                        plain(wout_hi[:, ds(k, 1), :].rearrange("p o c -> p (o c)")),
                                        ALU.subtract).then_inc(lo_ready, 1)

            with pool.Fori(0, N_MERGE // 4) as i:
                for j in range(4):
                    low(4 * i + j, j)
            for n in range(N_MERGE // 4 * 4, N_MERGE + 1):
                low(n, n % 4)
            with pool.Fori(0, KB // 2) as i:
                for j in range(2):
                    low_out(4 * i + (N_MERGE + 1 + 2 * j), (N_MERGE + 1 + 2 * j) % 4, 2 * i + j)
                    low(4 * i + (N_MERGE + 2 + 2 * j), (N_MERGE + 2 + 2 * j) % 4)
            with pool.Fori(0, (N_BLOCKS - N_UP - 1) // 4) as i:
                for j in range(4):
                    low(4 * i + (N_UP + 1 + j), (N_UP + 1 + j) % 4)
            for n in range(N_UP + 1 + (N_BLOCKS - N_UP - 1) // 4 * 4, N_BLOCKS):
                low(n, n % 4)

        @block.scalar
        def _(act):
            def table(index):
                act.add_instruction(mybir.InstLoadActFuncSet(
                    name=nc.get_next_instruction_name(), act_func_set_id=index,
                    engine=mybir.EngineType.Activation))

            def arrived(n, slot, turn):
                act.wait_ge(raw_in[slot], turn * 16 + 16)

            def high(n, slot, turn, used):
                arrived(n, slot, turn)
                if used is not None:
                    act.wait_ge(block_done, used)
                nc.scalar.activation(w_hi[:, slot, :], w_raw[:, slot, :], ACT.Copy).then_inc(hi_ready, 1)

            def high_in_order(n):
                high(n, n % 4, n // 4, n - 3 if n >= 4 else None)

            table(SET_LN_EXP)
            for k in range(KB):
                act.wait_ge(x_in[k], 16)
                nc.scalar.activation(xT_hi[:, k, :], xT_raw[:, k, :], ACT.Copy).then_inc(xhi_ready, 1)
                high_in_order(k)
            for n in range(N_F, N_F + 3):
                high_in_order(n)
            high_in_order(N_F + 3)
            act.wait_ge(block_done, N_F + 1)
            act.wait_ge(const_in, 48)
            nc.scalar.activation(f_e[:], bank(0), ACT.Abs, bias=col[:, COL_F:COL_F + 1]).then_inc(f_absed, 1)
            act.wait_ge(f_absed, 1)
            nc.scalar.activation(f_e[:], f_e[:], ACT.Exp, scale=-1.0).then_inc(f_exped, 1)
            act.wait_ge(f_exped, 1)
            nc.scalar.activation(f_e[:], f_e[:], ACT.Ln, bias=1.0).then_inc(f_lned, 1)

            def read_qk(pair, j, bank_, done, free):
                act.wait_ge(block_done, done)
                if free is not None:
                    act.wait_ge(qk_split, free)
                bias = (q_bias if j % 2 == 0 else col)[:, ds(pair * 4 + j, 1)]
                nc.scalar.activation(qk_t[:, j % 2, :], bank(bank_), ACT.Identity, bias=bias,
                                     scale=HEAD_DIM ** -0.5 if j % 2 == 0 else 1.0).then_inc(block_read, 1)

            act.wait_ge(const_ready, 1)
            for j in range(4):
                high_in_order(N_QK0 + j + 3)
                read_qk(0, j, 6 + j % 2, N_QK0 + j + 1, j - 1 if j >= 2 else None)

            def read_block(pair, place, blocks, n):
                kind, index, bank_ = blocks[place]
                if kind == "gate":
                    act.wait_ge(block_done, n + 1)
                    nc.scalar.activation(g_all[:, ds(index, 1), :].rearrange("p o c -> p (o c)"), bank(bank_),
                                         ACT.Identity, bias=col[:, ds(COL_G + index, 1)]).then_inc(block_read, 1)
                else:
                    read_qk(pair + 1, index, bank_, n + 1, (pair + 1) * 4 + (index - 1))

            def half(pair, e, blocks, n0, highs):
                h = pair * 2 + e
                at_place = {pl: n0 + k for k, pl in enumerate(sorted(blocks))}
                act.wait_ge(sb_mixed, h + FREE)
                act.wait_ge(sb_scored, h + 1)
                nc.scalar.activation(sb_t[:], ps[:, SB_PS:SB_PS + FLAT], ACT.Abs).then_inc(sb_absed, 1)
                act.wait_ge(sb_absed, h + 1)
                nc.scalar.activation(sb_t[:], sb_t[:], ACT.Exp, scale=-1.0).then_inc(sb_exped, 1)
                act.wait_ge(sb_exped, h + 1)
                nc.scalar.activation(sb_t[:], sb_t[:], ACT.Ln, bias=1.0).then_inc(sb_lned, 1)
                if 0 in blocks:
                    highs(0)
                    read_block(pair, 0, blocks, at_place[0])
                act.wait_ge(fx_mixed, h + FREE)
                act.wait_ge(fx_maxed, h * SB + SB)
                for r in range(SB):
                    off, width = FX_OFF[r], P * (r + 1)
                    nc.scalar.activation(fx_p[:, off:off + width], ps[:, FX_PS + off:FX_PS + off + width], ACT.Exp,
                                         bias=fx_nmax[:, r:r + 1],
                                         accum_out=fx_sum[:, r:r + 1]).then_inc(fx_exped, 1)
                if 1 in blocks:
                    highs(1)
                    read_block(pair, 1, blocks, at_place[1])
                act.wait_ge(sb_summed, h + 1)
                nc.scalar.activation(sb_t[:], ps[:, SB_PS:SB_PS + FLAT], ACT.Exp).then_inc(sb_weighed, 1)
                if 2 in blocks:
                    highs(2)
                    read_block(pair, 2, blocks, at_place[2])
                act.wait_ge(fx_turned, h + 1)
                nc.scalar.activation(fx_hi[:], ps[:, FX_PS:FX_PS + FLAT], ACT.Copy).then_inc(fx_w_hi, 1)
                if 3 in blocks:
                    highs(3)
                    read_block(pair, 3, blocks, at_place[3])
                for b, mixed in ((0, sb_mixed), (1, fx_mixed)):
                    act.wait_ge(mixed, h + FREE + 1)
                    rows_ = slice(HEAD_DIM * e, HEAD_DIM * (e + 1))
                    nc.scalar.activation(oT_hi[rows_, ds(pair + PAIRS * b, 1), :].rearrange("p o c -> p (o c)"),
                                         ps[rows_, 512 * (6 + b):512 * (7 + b)], ACT.Copy).then_inc(o_hi_done[b], 1)

            act.sem_inc(sb_weighed, FREE)
            act.sem_inc(fx_exped, FREE * SB)
            with act.Fori(0, PAIRS - 1) as pair:
                for e in range(2):
                    n0 = pair * 8 + (N_PAIR + 4 * e)

                    def highs(place, n0=n0, e=e):
                        m = N_PAIR + 4 * e + place + 3
                        high(None, m % 4, pair * 2 + m // 4, pair * 8 + (m - 3))
                    half(pair, e, loop_blocks(pair)[e], n0, highs)
            for e in range(2):
                def highs(place, e=e):
                    n = N_LAST + 2 * e + (place // 2) + 3
                    if n <= N_MERGE:
                        high_in_order(n)
                half(PAIRS - 1, e, LAST_BLOCKS[e], N_LAST + 2 * e, highs)

            table(SET_SIGMOID)
            act.wait_ge(sb_mixed, HALVES + FREE)
            act.wait_ge(fx_mixed, HALVES + FREE)
            with act.Fori(0, KB // 2) as i:
                for j in range(2):
                    for b in range(2):
                        gate = g_all[:, ds(2 * i + (j + KB * b), 1), :].rearrange("p o c -> p (o c)")
                        nc.scalar.activation(gate, gate, ACT.Sigmoid).then_inc(gated, 1)
                    m = N_MERGE + 1 + 2 * j
                    arrived(None, m % 4, i + m // 4)
                    nc.scalar.activation(wout_hi[:, ds(2 * i + j, 1), :].rearrange("p o c -> p (o c)"),
                                         w_raw[:, m % 4, :], ACT.Copy).then_inc(hi_ready, 1)
                    high(None, (m + 1) % 4, i + (m + 1) // 4, 2 * i + (USED_PAIRS + j))

            def root(k):
                act.wait_ge(ln_vared, k + 1)
                nc.scalar.activation(ln_log[:], ln_var[:], ACT.Ln).then_inc(ln_logged, 1)
                act.wait_ge(ln_logged, k + 1)
                nc.scalar.activation(ln_r0[:], ln_log[:], ACT.Exp, scale=-0.5).then_inc(ln_rooted, 1)

            table(SET_LN_EXP)
            for n in range(N_UP + 1, N_UP + 3):
                high(n, n % 4, n // 4, None)

            def x1_high(s):
                act.wait_ge(x1_turned, s + 1)
                for half_ in range(2):
                    nc.scalar.activation(x1T_hi[:, 4 * half_:4 * half_ + 4, P * s:P * (s + 1)],
                                         bank(2 * s + half_).rearrange("p (k c) -> p k c", c=P),
                                         ACT.Copy).then_inc(x1_hi_done, 1)

            for s in range(SB):
                root(s)
                if s > 0:
                    x1_high(s - 1)
            x1_high(SB - 1)

            table(SET_GELU)
            with act.Fori(0, FB // 2) as i:
                for j in range(2):
                    f = 2 * i + j
                    for g in range(2):
                        m = N_UP + 2 * j + g + 3
                        high(None, m % 4, i + m // 4, 4 * i + (m - W_SLOTS - UP_LAG + 1))
                    act.wait_ge(block_done, 4 * i + (USED_MERGE + 2 * j + 1))
                    act.wait_ge(act_ready, f + 1)
                    nc.scalar.activation(conv[:, j, :], bank(2 * j), ACT.Identity,
                                         bias=col[:, ds(COL_CB + f, 1)],
                                         scale=col[:, ds(f * CONV_WIDTH + (COL_CW + CONV_WIDTH - 1), 1)]
                                         ).then_inc(cv_biased, 1)
                    act.wait_ge(cv_done, f + 1)
                    nc.scalar.activation(gelu[:, j, :], conv[:, j, :], ACT.Gelu).then_inc(gelu_done, 1)

            table(SET_LN_EXP)

            def a_high(f, slot):
                act.wait_ge(act_ready, f + (FREE_ACT + 1))
                act.wait_ge(block_done, f + (USED_UP - W_SLOTS + 1))
                nc.scalar.activation(a_hi[:, slot, :], aT[:, ds(f, 1), :].rearrange("p o c -> p (o c)"),
                                     ACT.Copy).then_inc(a_hi_done, 1)

            a_high(0, 0)
            a_high(1, 1)
            for f in range(2):
                a_high(f + 2, f + 2)
                n = N_DOWN + f + 3
                high(n, n % 4, n // 4, n - W_SLOTS - UP_LAG + 1)
            with act.Fori(0, (FB - RESIDENT - 2) // 4) as i:
                for j in range(4):
                    f = 4 * i + (j + 2)
                    a_high(f + 2, j)
                    m = N_DOWN + 2 + j + 3
                    high(None, m % 4, i + m // 4, 4 * i + (m - W_SLOTS - UP_LAG + 1))
            for f in range(FB - RESIDENT, FB):
                if f + 2 < FB:
                    a_high(f + 2, (f + 2) % 4)
                n = N_DOWN + f + 3
                if n < N_BLOCKS:
                    high(n, n % 4, n // 4, n - W_SLOTS - UP_LAG + 1)
            for s in range(SB):
                root(SB + s)

        @block.vector
        def _(dve):
            def split_lo(out_lo, whole, part_hi):
                return nc.vector.tensor_tensor(out_lo, whole, plain(part_hi), ALU.subtract)

            for k in range(KB):
                dve.wait_ge(xhi_ready, k + 1)
                split_lo(xT_lo[:, k, :], xT_raw[:, k, :], xT_hi[:, k, :]).then_inc(xlo_ready, 1)
            dve.wait_ge(const_in, 48)
            nc.vector.tensor_scalar(q_bias[:], col[:, COL_QK:COL_QK + 4 * PAIRS], HEAD_DIM ** -0.5, None,
                                    ALU.mult)
            nc.vector.tensor_copy(neg_tri[:], sq_raw[:, 1, :])
            nc.vector.tensor_copy(neg_one[:], sq_raw[:, 2, :])
            nc.vector.tensor_copy(ident_bf[:], sq_raw[:, 0, :])
            nc.vector.tensor_copy(mask_bf[:], sq_raw[:, 3:5, :])
            nc.vector.memset(f_zero[:], 0.0).then_inc(const_ready, 1)
            dve.wait_ge(vb_in, 16)
            dve.wait_ge(block_done, KB)
            for b in V_READ:
                s, br = b // 2, b % 2
                nc.vector.tensor_tensor(v_all[:, s, 512 * br:512 * (br + 1)], bank(b),
                                        vb_row[:, 512 * br:512 * (br + 1)], ALU.add).then_inc(v_ready, 1)

            dve.wait_ge(block_done, N_F + 1)
            dve.wait_ge(f_absed, 1)
            nc.vector.tensor_scalar(f_min[:], bank(0), col[:, COL_F:COL_F + 1], 0.0, ALU.add,
                                    ALU.min).then_inc(f_mined, 1)
            dve.wait_ge(f_mined, 1)
            dve.wait_ge(f_lned, 1)
            nc.vector.tensor_tensor(f_log[:], f_min[:], f_e[:], ALU.subtract).then_inc(f_logged, 1)
            dve.wait_ge(f_logged, 1)
            nc.vector.tensor_tensor_scan(f_cum[:], f_log[:], f_zero[:], 0.0, ALU.add, ALU.add).then_inc(f_cumed, 1)
            dve.wait_ge(f_cumed, 1)
            nc.vector.tensor_copy(f_hi[:], f_cum[:]).then_inc(f_split, 1)
            dve.wait_ge(f_split, 1)
            split_lo(f_lo[:], f_cum[:], f_hi[:]).then_inc(f_lo_done, 1)
            dve.wait_ge(f_lo_done, 1)
            for k, (side, c0) in enumerate(((f_rhs, COL_SEL), (f_lhs, COL_SEL + 3))):
                if k:
                    dve.wait_ge(f_ready, k)
                nc.vector.tensor_scalar(f_tmp[:], plain(f_lo[:]), col[:, c0 + 1:c0 + 2], col[:, c0 + 2:c0 + 3],
                                        ALU.mult, ALU.add).then_inc(f_part, 1)
                dve.wait_ge(f_part, k + 1)
                nc.vector.scalar_tensor_tensor(side[:], plain(f_hi[:]), col[:, c0:c0 + 1], f_tmp[:], ALU.mult,
                                               ALU.add).then_inc(f_ready, 1)
            dve.wait_ge(f_ready, 2)

            def split_qk(j, m, read):
                dve.wait_ge(block_read, read)
                nc.vector.tensor_copy(qk_hi[:, j, :], qk_t[:, j % 2, :]).then_inc(qk_hi_done, 1)
                dve.wait_ge(qk_hi_done, m + 1)
                split_lo(qk_lo[:, j, :], qk_t[:, j % 2, :], qk_hi[:, j, :]).then_inc(qk_split, 1)

            for j in range(4):
                split_qk(j, j, j + 1)

            def split_next(pair, j):
                if j < 2:
                    dve.wait_ge(sb_scored, pair * 2 + 2)
                else:
                    dve.wait_ge(fx_scored, pair * 2 + (2 + FREE))
                split_qk(j, pair * 4 + (4 + j), pair * 8 + (4 + 4 + j + 1))

            def half(pair, e, qk):
                h = pair * 2 + e
                dve.wait_ge(fx_scored, h + FREE)
                nc.vector.tensor_scalar(f_sel[:], f_lhs[:], col[:, ds(COL_MASK + h, 1)], None,
                                        ALU.mult).then_inc(sel_ready, 1)
                if e == 0:
                    dve.wait_ge(sb_mixed, h + FREE)
                    dve.wait_ge(fx_mixed, h + FREE)
                    for b in range(2):
                        dve.wait_ge(v_ready, 2 * SB)
                        v_pair = v_all[:, :, ds(pair * P + D_SB * b, P)]
                        nc.vector.tensor_copy(v_hi[:, b, :, :], v_pair).then_inc(v_hi_done, 1)
                        dve.wait_ge(v_hi_done, pair * 2 + (b + 1))
                        split_lo(v_lo[:, b, :, :], v_pair, v_hi[:, b, :, :]).then_inc(v_split, 1)
                dve.wait_ge(sb_lned, h + 1)
                nc.vector.scalar_tensor_tensor(sb_t[:], ps[:, SB_PS:SB_PS + FLAT], 0.0, sb_t[:], ALU.max,
                                               ALU.add).then_inc(sb_soft, 1)
                dve.wait_ge(sb_soft, h + 1)
                nc.vector.tensor_copy(sb_hi[:], sb_t[:]).then_inc(sb_soft_hi, 1)
                dve.wait_ge(sb_soft_hi, h + 1)
                split_lo(sb_lo[:], sb_t[:], sb_hi[:]).then_inc(sb_soft_split, 1)
                dve.wait_ge(fx_scored, h + FREE + 1)
                dve.wait_ge(fx_exped, h * SB + FREE * SB)
                for r in range(SB):
                    off, width = FX_OFF[r], P * (r + 1)
                    nc.vector.tensor_reduce(fx_nmax[:, r:r + 1], ps[:, FX_PS + off:FX_PS + off + width], AX.X,
                                            ALU.max, negate=True).then_inc(fx_maxed, 1)
                if qk:
                    split_next(pair, 0)
                dve.wait_ge(fx_exped, h * SB + (FREE + 1) * SB)
                dve.wait_ge(fx_normed, h * SB + FREE * SB)
                nc.vector.reciprocal(fx_rec[:], fx_sum[:]).then_inc(fx_inverted, 1)
                dve.wait_ge(fx_inverted, h + 1)
                for r in range(SB):
                    off, width = FX_OFF[r], P * (r + 1)
                    nc.vector.tensor_scalar(fx_p[:, off:off + width], fx_p[:, off:off + width],
                                            fx_rec[:, r:r + 1], None, ALU.mult).then_inc(fx_normed, 1)
                if qk:
                    split_next(pair, 1)
                dve.wait_ge(sb_weighed, h + FREE + 1)
                nc.vector.tensor_copy(sb_hi[:], sb_t[:]).then_inc(sb_w_hi, 1)
                dve.wait_ge(sb_w_hi, h + 1)
                split_lo(sb_lo[:], sb_t[:], sb_hi[:]).then_inc(sb_w_split, 1)
                if qk:
                    split_next(pair, 2)
                dve.wait_ge(fx_w_hi, h + 1)
                split_lo(fx_lo[:], ps[:, FX_PS:FX_PS + FLAT], fx_hi[:]).then_inc(fx_w_split, 1)
                if qk:
                    split_next(pair, 3)
                for b in range(2):
                    dve.wait_ge(o_hi_done[b], h + 1)
                    rows_ = slice(HEAD_DIM * e, HEAD_DIM * (e + 1))
                    where = (rows_, ds(pair + PAIRS * b, 1))
                    last = split_lo(oT_lo[where].rearrange("p o c -> p (o c)"),
                                    ps[rows_, 512 * (6 + b):512 * (7 + b)],
                                    oT_hi[where].rearrange("p o c -> p (o c)"))
                    last.then_inc(o_split[b], 1)

            dve.sem_inc(fx_normed, FREE * SB)
            dve.sem_inc(fx_w_split, FREE)
            dve.sem_inc(o_split[0], FREE)
            dve.sem_inc(o_split[1], FREE)
            with dve.Fori(0, PAIRS - 1) as pair:
                for e in range(2):
                    half(pair, e, e == 1)
            for e in range(2):
                half(PAIRS - 1, e, False)
            dve.wait_ge(o_split[0], HALVES + FREE)
            dve.wait_ge(o_split[1], HALVES + FREE)
            dve.sem_inc(merged, FREE_MERGE)

            with dve.Fori(0, 2) as i:
                for j in range(4):
                    d = 4 * i + j
                    dve.wait_ge(block_done, d + (USED_PAIRS + 1))
                    dve.wait_ge(gated, d * 2 + 2)
                    dve.wait_ge(merged, d + FREE_MERGE)
                    for b, done in ((0, mg_a), (1, mg_b)):
                        nc.vector.tensor_tensor(mg_t[:, b, :], bank(MERGE_BANKS[j] + b),
                                                g_all[:, ds(d + KB * b, 1), :].rearrange("p o c -> p (o c)"),
                                                ALU.mult).then_inc(done, 1)
                    dve.wait_ge(mg_a, d + 1)
                    dve.wait_ge(mg_b, d + 1)
                    nc.vector.tensor_tensor(mg_t[:, 0, :], mg_t[:, 0, :], mg_t[:, 1, :], ALU.add).then_inc(mg_sum, 1)
                    dve.wait_ge(mg_sum, d + 1)
                    m_hi = mT_hi[:, ds(d, 1), :].rearrange("p o c -> p (o c)")
                    nc.vector.tensor_copy(m_hi, mg_t[:, 0, :]).then_inc(mg_hi, 1)
                    dve.wait_ge(mg_hi, d + 1)
                    split_lo(mT_lo[:, ds(d, 1), :].rearrange("p o c -> p (o c)"), mg_t[:, 0, :],
                             m_hi).then_inc(merged, 1)

            def layer_norm(s, k, banks, gain, shift):
                for half_ in range(2):
                    part = x1[:, s, 512 * half_:512 * (half_ + 1)]
                    nc.vector.scalar_tensor_tensor(part, part, ALPHA, bank(banks[half_]), ALU.mult,
                                                   ALU.add).then_inc(ln_added, 1)
                for half_ in range(2):
                    dve.wait_ge(ln_added, 2 * k + half_ + 1)
                    nc.vector.bn_stats(bn_parts[:, half_, :],
                                       x1[:, s, 512 * half_:512 * (half_ + 1)]).then_inc(ln_stated, 1)
                dve.wait_ge(ln_stated, 2 * k + 2)
                nc.vector.bn_aggr(bn_mv[:], bn_parts[:].rearrange("p a b -> p (a b)")).then_inc(ln_aggred, 1)
                dve.wait_ge(ln_aggred, k + 1)
                nc.vector.tensor_scalar(ln_var[:], bn_mv[:, 1:2], LN_EPS, None, ALU.add).then_inc(ln_vared, 1)
                dve.wait_ge(ln_vared, k + 1)
                dve.wait_ge(ln_rooted, k + 1)
                nc.vector.scalar_tensor_tensor(ln_nt[:], ln_r0[:], ln_r0[:], ln_var[:], ALU.mult,
                                               ALU.mult).then_inc(ln_newton, 1)
                dve.wait_ge(ln_newton, k + 1)
                nc.vector.tensor_scalar(ln_nt[:], ln_nt[:], -0.5, 1.5, ALU.mult, ALU.add).then_inc(ln_halved, 1)
                dve.wait_ge(ln_halved, k + 1)
                nc.vector.tensor_tensor(ln_r[:], ln_nt[:], ln_r0[:], ALU.mult).then_inc(ln_scale, 1)
                dve.wait_ge(ln_scale, k + 1)
                nc.vector.tensor_scalar(x1[:, s, :], x1[:, s, :], bn_mv[:, 0:1], ln_r[:], ALU.subtract,
                                        ALU.mult).then_inc(ln_normed, 1)
                dve.wait_ge(ln_normed, k + 1)
                nc.vector.tensor_tensor(x1[:, s, :], x1[:, s, :], ln_rows[:, gain, :], ALU.mult).then_inc(ln_gained, 1)
                dve.wait_ge(ln_gained, k + 1)
                nc.vector.tensor_tensor(x1[:, s, :], x1[:, s, :], ln_rows[:, shift, :], ALU.add).then_inc(ln_done, 1)

            def x1_low(s):
                for half_ in range(2):
                    dve.wait_ge(x1_hi_done, 2 * s + half_ + 1)
                    where = (slice(None), slice(4 * half_, 4 * half_ + 4), slice(P * s, P * (s + 1)))
                    split_lo(x1T_lo[where], bank(2 * s + half_).rearrange("p (k c) -> p k c", c=P),
                             x1T_hi[where]).then_inc(x1_split, 1)

            dve.wait_ge(row_in, 64)
            for s in range(SB):
                dve.wait_ge(tok_in[s], 16)
                dve.wait_ge(out_done, s + 1)
                layer_norm(s, s, (2 * s, 2 * s + 1), 0, 1)
                if s > 0:
                    x1_low(s - 1)
            x1_low(SB - 1)
            dve.wait_ge(x1_split, 2 * SB)
            dve.sem_inc(act_ready, FREE_ACT)

            with dve.Fori(0, FB // 2) as i:
                for j in range(2):
                    f = 2 * i + j
                    for t, (before, after) in ((1, (cv_biased, cv_one)), (2, (cv_one, cv_done))):
                        dve.wait_ge(before, f + 1)
                        nc.vector.scalar_tensor_tensor(
                            conv[:, j, t:SEQ], ps[:, 512 * 2 * j:512 * (2 * j + 1) - t],
                            col[:, ds(f * CONV_WIDTH + (COL_CW + CONV_WIDTH - 1 - t), 1)], conv[:, j, t:SEQ],
                            ALU.mult, ALU.add).then_inc(after, 1)
                    dve.wait_ge(gelu_done, f + 1)
                    dve.wait_ge(block_done, 4 * i + (USED_MERGE + 2 * j + 2))
                    nc.vector.tensor_tensor(aT[:, ds(f, 1), :].rearrange("p o c -> p (o c)"), bank(2 * j + 1),
                                            gelu[:, j, :], ALU.mult).then_inc(act_ready, 1)

            def a_low(f, slot):
                dve.wait_ge(a_hi_done, f + 1)
                split_lo(a_lo[:, slot, :], aT[:, ds(f, 1), :].rearrange("p o c -> p (o c)"),
                         a_hi[:, slot, :]).then_inc(a_split, 1)

            for f in range(2):
                a_low(f, f)
            with dve.Fori(0, (FB - 2) // 4) as i:
                for j in range(4):
                    a_low(4 * i + (j + 2), (j + 2) % 4)
            for s in range(SB):
                dve.wait_ge(out_done, SB + s + 1)
                layer_norm(s, SB + s, DOWN_BANKS[s], 2, 3)

        @block.tensor
        def _(pe):
            def product(out_, lhs, rhs, start=False, stop=False):
                return nc.tensor.matmul(out_, lhs, rhs, start=start, stop=stop, skip_group_check=True)

            def split_product(out_, l_hi, l_lo, r_hi, r_lo, start, stop):
                product(out_, l_hi, r_hi, start=start)
                product(out_, l_hi, r_lo)
                return product(out_, l_lo, r_hi, stop=stop)

            def weight_ready(n):
                pe.wait_ge(lo_ready, n + 1)

            def column_block(n, slot, bank_):
                weight_ready(n)
                for k in range(KB):
                    w = (slice(None), slot, slice(P * k, P * (k + 1)))
                    last = split_product(bank(bank_), w_hi[w], w_lo[w], xT_hi[:, k, :], xT_lo[:, k, :],
                                         k == 0, k == KB - 1)
                last.then_inc(block_done, 1)

            for k in range(KB):
                pe.wait_ge(xlo_ready, k + 1)
                weight_ready(k)
                for b in range(2 * SB):
                    s, br = b // 2, b % 2
                    xs = (slice(None), k, slice(P * s, P * (s + 1)))
                    ws = (slice(None), k % W_SLOTS, slice(512 * br, 512 * (br + 1)))
                    last = split_product(bank(b), xT_hi[xs], xT_lo[xs], w_hi[ws], w_lo[ws], k == 0, k == KB - 1)
                last.then_inc(block_done, 1)
            pe.wait_ge(v_ready, 1)
            column_block(N_F, N_F % 4, 0)
            for j in range(4):
                if j < 2:
                    pe.wait_ge(v_ready, 2 + j)
                else:
                    pe.wait_ge(block_read, j - 1)
                column_block(N_QK0 + j, (N_QK0 + j) % 4, 6 + j % 2)

            def half(pair, e, blocks, turn, first):
                h = pair * 2 + e
                n0 = turn + first
                b0 = turn + (first - N_QK0)
                hd = slice(HEAD_DIM * e, HEAD_DIM * (e + 1))
                order = sorted(blocks)

                def fill(place):
                    if place not in blocks:
                        return
                    k = order.index(place)
                    bank_ = blocks[place][2]
                    if k < 2:
                        pe.wait_ge(o_split[bank_ - 6], h + FREE)
                        pe.wait_ge(block_read, 3 + bank_ - 6)
                    else:
                        pe.wait_ge(block_read, b0 + (k - 1))
                    column_block(n0 + k, (first + k) % 4, bank_)

                pe.wait_ge(qk_split, pair * 4 + 2)
                pe.wait_ge(sb_weighed, h + FREE)
                pe.wait_ge(v_ready, 2 * SB)
                pe.wait_ge(f_mined, 1)
                pe.wait_ge(f_absed, 1)
                for k_part, q_part, opens in ((qk_hi, qk_hi, True), (qk_hi, qk_lo, False), (qk_lo, qk_hi, False)):
                    for r in (0, 1, 2, 3):
                        o = SB_PS + SB_OFF[r]
                        product(ps[:, o:o + P * (SB - r)], k_part[hd, 1, P * r:P * (r + 1)],
                                q_part[hd, 0, P * r:SEQ], start=opens and r < 3)
                for r in range(SB):
                    o = SB_PS + SB_OFF[r]
                    last = product(ps[:, o:o + P], ident_bf[:], mask_bf[:, 0, :])
                last.then_inc(sb_scored, 1)
                fill(0)
                pe.wait_ge(qk_split, pair * 4 + 4)
                pe.wait_ge(fx_w_split, h + FREE)
                pe.wait_ge(sel_ready, h + 1)
                for r in (3, 2, 1, 0):
                    o, width = FX_PS + FX_OFF[r], P * (r + 1)
                    product(ps[:, o:o + width], f_sel[:, P * r:P * (r + 1)], f_rhs[:, 0:width], start=r > 0)
                for q_part, k_part in ((qk_hi, qk_hi), (qk_hi, qk_lo), (qk_lo, qk_hi)):
                    for r in (3, 2, 1, 0):
                        o, width = FX_PS + FX_OFF[r], P * (r + 1)
                        product(ps[:, o:o + width], q_part[hd, 2, P * r:P * (r + 1)], k_part[hd, 3, 0:width])
                for r in range(SB):
                    o = FX_PS + FX_OFF[r] + P * r
                    last = product(ps[:, o:o + P], ident_bf[:], mask_bf[:, 1, :])
                last.then_inc(fx_scored, 1)
                fill(1)
                pe.wait_ge(sb_soft_split, h + 1)
                for part in (sb_hi, sb_lo):
                    for r in range(SB):
                        o = SB_OFF[r]
                        product(ps[:, SB_PS + o:SB_PS + o + P * (SB - r)], neg_tri[:], part[:, o:o + P * (SB - r)])
                for part in (sb_hi, sb_lo):
                    for r in range(SB - 1):
                        for r2 in range(r + 1, SB):
                            o, o2, width = SB_OFF[r] + P * (r2 - r), SB_OFF[r2], P * (SB - r2)
                            last = product(ps[:, SB_PS + o:SB_PS + o + width], neg_one[:], part[:, o2:o2 + width])
                last.then_inc(sb_summed, 1)
                fill(2)
                pe.wait_ge(fx_normed, h * SB + (FREE + 1) * SB)
                for r in range(SB):
                    for c in range(r + 1):
                        o = FX_PS + SB_OFF[c] + P * (r - c)
                        last = nc.tensor.transpose(ps[:, o:o + P], fx_p[:, FX_OFF[r] + P * c:FX_OFF[r] + P * (c + 1)],
                                                   ident[:])
                last.then_inc(fx_turned, 1)
                fill(3)
                pe.wait_ge(v_split, pair * 2 + 2)
                for b, split, ready, hi, lo, mixed in ((0, sb_w_split, h + 1, sb_hi, sb_lo, sb_mixed),
                                                       (1, fx_w_split, h + FREE + 1, fx_hi, fx_lo, fx_mixed)):
                    pe.wait_ge(split, ready)
                    pe.wait_ge(block_read, b0 + (len(order) - 1 + b))
                    for r in range(SB):
                        o = SB_OFF[r]
                        span = (slice(None), slice(o, o + P * (SB - r)))
                        last = split_product(ps[:, 512 * (6 + b) + P * r:512 * (7 + b)], v_hi[:, b, r, :],
                                             v_lo[:, b, r, :], hi[span], lo[span], r == 0, r == SB - 1)
                    last.then_inc(mixed, 1)

            pe.sem_inc(sb_mixed, FREE)
            pe.sem_inc(fx_mixed, FREE)
            pe.sem_inc(fx_scored, FREE)
            with pe.Fori(0, PAIRS - 1) as pair:
                for e in range(2):
                    half(pair, e, loop_blocks(pair)[e], pair * 8, N_PAIR + 4 * e)
            for e in range(2):
                half(PAIRS - 1, e, LAST_BLOCKS[e], 0, N_LAST + 2 * e)

            pe.wait_ge(o_split[0], HALVES + FREE)
            pe.wait_ge(o_split[1], HALVES + FREE)
            with pe.Fori(0, 2) as i:
                for j in range(4):
                    weight_ready(8 * i + (N_MERGE + 2 * j))
                    pe.wait_ge(merged, 4 * i + (j + 1))
                    for k in range(KB):
                        w = (slice(None), (N_MERGE + 2 * j) % 4, slice(P * k, P * (k + 1)))
                        last = split_product(bank(MERGE_BANKS[j] + k // PAIRS), w_hi[w], w_lo[w], oT_hi[:, k, :],
                                             oT_lo[:, k, :], k % PAIRS == 0, k % PAIRS == PAIRS - 1)
                    last.then_inc(block_done, 1)

            def turn(s):
                pe.wait_ge(ln_done, s + 1)
                for k in range(KB):
                    last = nc.tensor.transpose(bank(2 * s + k // 4)[:, P * (k % 4):P * (k % 4 + 1)],
                                               x1[:, s, P * k:P * (k + 1)], ident[:])
                last.then_inc(x1_turned, 1)

            pe.wait_ge(merged, KB + FREE_MERGE)
            weight_ready(N_UP - 1)
            for s in range(SB):
                for half_ in range(2):
                    for k in range(KB):
                        ms = (slice(None), k, slice(P * s, P * (s + 1)))
                        ws = (slice(None), k, slice(512 * half_, 512 * (half_ + 1)))
                        last = split_product(bank(2 * s + half_), mT_hi[ms], mT_lo[ms], wout_hi[ws], wout_lo[ws],
                                             k == 0, k == KB - 1)
                last.then_inc(out_done, 1)
                if s > 0:
                    turn(s - 1)
            turn(SB - 1)

            pe.wait_ge(x1_split, 2 * SB)
            with pe.Fori(0, FB // 2) as i:
                for j in range(2):
                    pe.wait_ge(act_ready, 2 * i + (j + 1))
                    for g in range(2):
                        m = N_UP + 2 * j + g
                        weight_ready(4 * i + m)
                        for k in range(KB):
                            w = (slice(None), m % 4, slice(P * k, P * (k + 1)))
                            last = split_product(bank(2 * j + g), w_hi[w], w_lo[w], x1T_hi[:, k, :],
                                                 x1T_lo[:, k, :], k == 0, k == KB - 1)
                        last.then_inc(block_done, 1)

            def down(s, f, slot_a, slot_w):
                for half_ in range(2):
                    as_ = (slice(None), slot_a, slice(P * s, P * (s + 1)))
                    ws = (slice(None), slot_w, slice(512 * half_, 512 * (half_ + 1)))
                    last = split_product(bank(DOWN_BANKS[s][half_]), a_hi[as_], a_lo[as_], w_hi[ws], w_lo[ws],
                                         isinstance(f, int) and f == 0, isinstance(f, int) and f == FB - 1)
                return last

            def down_block(f, slot_a, slot_w):
                pe.wait_ge(a_split, f + 1)
                weight_ready(f + N_DOWN)
                for s in range(SB):
                    if isinstance(f, int) and f == 0 and s >= 2:
                        pe.wait_ge(act_ready, FREE_ACT + FB - 2 + s - 1)
                    last = down(s, f, slot_a, slot_w)
                last.then_inc(block_done, 1)

            for f in range(2):
                down_block(f, f, (N_DOWN + f) % 4)
            with pe.Fori(0, (FB - RESIDENT - 2) // 4) as i:
                for j in range(4):
                    down_block(4 * i + (j + 2), (j + 2) % 4, (N_DOWN + 2 + j) % 4)
            pe.wait_ge(a_split, FB)
            weight_ready(N_BLOCKS - 1)
            for s in range(SB):
                for f in range(FB - RESIDENT, FB):
                    last = down(s, f, f % 4, (N_DOWN + f) % 4)
                last.then_inc(out_done, 1)


V_READ = (0, 6, 7, 1, 2, 3, 4, 5)
MERGE_BANKS = (6, 0, 2, 4)
DOWN_BANKS = ((4, 5), (6, 7), (0, 1), (2, 3))
SET_SIGMOID, SET_LN_EXP, SET_GELU = 2, 6, 10


def loop_blocks(pair):
    gates = {pl: ("gate", pair * 4 + pl, 6 + pl % 2) for pl in range(4)}
    next_qk = {pl: ("qk", pl, 6 + pl % 2) for pl in range(4)}
    return gates, next_qk


LAST_BLOCKS = [{0: ("gate", NG - 4 + 2 * e, 6), 2: ("gate", NG - 3 + 2 * e, 7)} for e in range(2)]


def kernel(x, w_in, b_in, w_proj_sb, w_proj_fox, w_out, ln1_g, ln1_b, w_up, w_conv, b_conv, w_down, ln2_g, ln2_b):
    import numpy as np
    import concourse.bacc as bacc
    from concourse.bass_utils import run_bass_kernel_spmd

    x2, w_in, b_in = np.asarray(x)[0], np.asarray(w_in)[0], np.asarray(b_in)[0]
    w_out, w_up, w_down = np.asarray(w_out)[0], np.asarray(w_up)[0], np.asarray(w_down)[0]
    w_proj = np.concatenate([np.asarray(w_proj_sb)[0], np.asarray(w_proj_fox)[0]], axis=0)
    w_conv, b_conv = np.asarray(w_conv)[0], np.asarray(b_conv)[0]
    q_sb, k_sb, v_sb, q_fx, k_fx, v_fx, f0, g0 = (0, 512, 1024, 1536, 2048, 2560, 3072, 3072 + N_FORGET)

    def columns(w, start):
        return w[:, start:start + P].reshape(KB, P, P).transpose(1, 0, 2).reshape(P, KB * P)

    head_of = (np.arange(P) // 4) % N_FORGET
    v_cols = np.concatenate([w_in[:, v_sb:v_sb + D_SB], w_in[:, v_fx:v_fx + D_FOX]], axis=1)
    stream = [v_cols[P * k:P * (k + 1)] for k in range(KB)]
    stream.append(columns(w_in[:, f0:f0 + N_FORGET][:, head_of], 0))
    qk = lambda p: [columns(w_in, c + P * p) for c in (q_sb, k_sb, q_fx, k_fx)]
    gate = lambda g: columns(w_in, g0 + P * g)
    stream += qk(0)
    for p in range(PAIRS - 1):
        stream += [gate(4 * p + j) for j in range(4)] + qk(p + 1)
    stream += [gate(g) for g in range(NG - 4, NG)]
    for d in range(KB):
        stream += [columns(w_proj, P * d), w_out[P * d:P * (d + 1)]]
    for f in range(FB):
        stream += [columns(w_up, P * f), columns(w_up, D_FF + P * f)]
    stream += [w_down[P * f:P * (f + 1)] for f in range(FB)]
    assert len(stream) == N_BLOCKS

    row = np.arange(P)
    sel = np.zeros((P, 6 + N_FORGET), np.float32)
    for c, r, value in ((0, 0, -1), (1, 1, -1), (2, 2, 1), (2, 3, 1), (3, 2, 1), (4, 3, 1), (5, 0, 1), (5, 1, 1)):
        sel[row % 4 == r, c] = value
    for h in range(N_FORGET):
        sel[(row < 4 * N_FORGET) & (row // 4 == h), 6 + h] = 1
    vectors = [b_in[c + P * p:c + P * (p + 1)] for p in range(PAIRS) for c in (q_sb, k_sb, q_fx, k_fx)]
    vectors += [b_in[g0 + P * g:g0 + P * (g + 1)] for g in range(NG)]
    vectors += [b_in[f0:f0 + N_FORGET][head_of]]
    vectors += [w_conv[t, P * f:P * (f + 1)] for f in range(FB) for t in range(CONV_WIDTH)]
    vectors += [b_conv[P * f:P * (f + 1)] for f in range(FB)]
    cols = np.concatenate([np.stack(vectors, axis=1), sel], axis=1)
    v_bias = np.concatenate([b_in[v_sb:v_sb + D_SB], b_in[v_fx:v_fx + D_FOX]])
    rows = np.stack([v_bias] + [np.asarray(a)[0] for a in (ln1_g, ln1_b, ln2_g, ln2_b)])
    a, b = np.arange(P)[:, None], np.arange(P)[None, :]
    square = np.stack([a == b, -(a >= b).astype(np.float32), -np.ones((P, P)), -BIG * (a >= b), -BIG * (b > a)],
                      axis=1).astype(np.float32)
    arrays = {"xT_in": x2.T.reshape(KB, P, SEQ), "x_tok_in": x2, "w_stream_in": np.stack(stream), "cols_in": cols,
              "rows_in": rows, "square_in": square}
    arrays = {name: np.ascontiguousarray(value) for name, value in arrays.items()}

    nc = bacc.Bacc("TRN2", target_bir_lowering=False, num_devices=1)
    args = [nc.dram_tensor(name, value.shape, mybir.dt.from_np(value.dtype), kind="ExternalInput").ap()
            for name, value in arrays.items()]
    out = nc.dram_tensor("out_dram", (SEQ, D_MODEL), mybir.dt.float32, kind="ExternalOutput").ap()
    layer(nc, *args, out)
    result = run_bass_kernel_spmd(nc, [arrays], core_ids=[0])
    return result.results[0]["out_dram"].reshape(1, SEQ, D_MODEL)
```

```python
import concourse.bass as bass
from concourse import mybir
from contextlib import ExitStack

P = 128
D_MODEL = 1024
SEQ = 512
HEAD_DIM = 64
D_SB = 512
D_FOX = 512
N_FORGET = 8
D_FF = 2816
CONV_WIDTH = 3
LN_EPS = 1e-5
ALPHA = 2.0 ** 0.25

KB = D_MODEL // P
SB = SEQ // P
FB = D_FF // P
PAIRS = D_SB // P
HALVES = 2 * PAIRS
NG = 2 * KB
BIG = 1e30

N_F = KB
N_QK0 = N_F + 1
N_PAIR = N_QK0 + 4
N_LAST = N_PAIR + 8 * (PAIRS - 1)
N_MERGE = N_LAST + 4
N_UP = N_MERGE + KB
N_DOWN = N_UP + 2 * FB
N_BLOCKS = N_DOWN + FB
W_SLOTS = 4
RESIDENT = 5

COL_QK = 0
COL_G = COL_QK + 4 * PAIRS
COL_F = COL_G + NG
COL_CW = COL_F + 1
COL_CB = COL_CW + CONV_WIDTH * FB
COL_SEL = COL_CB + FB
COL_MASK = COL_SEL + 6
N_COLS = COL_MASK + N_FORGET

SB_OFF = [0, 640, 1024, 512]
FX_OFF = [896, 1024, 512, 0]
FLAT = 1280
SB_MASKED = [(0, 1), (512, 2), (1024, 1)]
FX_MASKED = [(384, 1), (768, 2), (1152, 1)]
LATER_OFF = [0, 3 * P]
LATER = 5 * P


def layer(nc, xT, x_tok, w_stream, w_out, cols, rows, square, out):
    f32, f32r, bf16 = mybir.dt.float32, mybir.dt.float32r, mybir.dt.bfloat16
    ACT, ALU, AX = mybir.ActivationFunctionType, mybir.AluOpType, mybir.AxisListType
    ds = bass.ds

    K = 1024
    area_w = (nc.sbuf_base + 63) // 64 * 64
    area_x, area_o, area_g = area_w + 32 * K, area_w + 64 * K, area_w + 96 * K
    area_a, area_c = area_w + 128 * K, area_w + 198 * K
    assert area_c + 5952 + 4 * K <= nc.sbuf_usable_end

    def at(name, shape, dt, offset):
        return nc.alloc_sbuf_tensor_at(name, shape, dt, offset=offset)

    w_raw = at("w_raw", [P, W_SLOTS, 1024], f32, area_w)
    w_lo = at("w_lo", [P, W_SLOTS, 1024], f32r, area_w)
    w_hi = at("w_hi", [P, W_SLOTS, 1024], f32r, area_w + 16 * K)
    xT_hi = at("xT_hi", [P, KB, SEQ], f32r, area_x)
    xT_lo = at("xT_lo", [P, KB, SEQ], f32r, area_x + 16 * K)
    mT_hi = at("mT_hi", [P, KB, SEQ], f32r, area_x)
    mT_lo = at("mT_lo", [P, KB, SEQ], f32r, area_x + 16 * K)
    r_raw = at("r_raw", [P, RESIDENT, 1024], f32, area_o)
    r_lo = at("r_lo", [P, RESIDENT, 1024], f32r, area_o)
    r_hi = at("r_hi", [P, RESIDENT, 1024], f32r, area_a + 44 * K)
    a_hi = at("a_hi", [P, W_SLOTS + 1, SEQ], f32r, area_x)
    a_lo = at("a_lo", [P, W_SLOTS + 1, SEQ], f32r, area_x + 10 * K)
    oT_hi = at("oT_hi", [P, KB, SEQ], f32r, area_o)
    oT_lo = at("oT_lo", [P, KB, SEQ], f32r, area_o + 16 * K)
    x1T_hi = at("x1T_hi", [P, KB, SEQ], f32r, area_o)
    x1T_lo = at("x1T_lo", [P, KB, SEQ], f32r, area_o + 16 * K)
    xT_raw = at("xT_raw", [P, KB, SEQ], f32, area_g)
    f_e = at("f_e", [P, SEQ], f32, area_g + 16 * K)
    f_min = at("f_min", [P, SEQ], f32, area_g + 18 * K)
    f_log = at("f_log", [P, SEQ], f32, area_g + 20 * K)
    f_zero = at("f_zero", [P, SEQ], f32, area_g + 22 * K)
    f_cum = at("f_cum", [P, SEQ], f32, area_g + 24 * K)
    f_hi = at("f_hi", [P, SEQ], f32r, area_g + 26 * K)
    f_lo = at("f_lo", [P, SEQ], f32r, area_g + 28 * K)
    f_tmp = at("f_tmp", [P, SEQ], f32, area_g + 30 * K)
    g_all = at("g_all", [P, NG, SEQ], f32, area_g)
    x1 = at("x1", [P, SB, D_MODEL], f32, area_g)
    ln_rows = at("ln_rows", [P, 4, D_MODEL], f32, area_g + 16 * K)
    v_all = at("v_all", [P, SB, 1024], f32, area_a)
    qk_hi = at("qk_hi", [P, 3, SEQ], f32r, area_a + 16 * K)
    qk_lo = at("qk_lo", [P, 3, SEQ], f32r, area_a + 22 * K)
    q_bias_rows = at("q_bias_rows", [P, 2, SEQ], f32r, area_a + 66 * K)
    k_bias_rows = at("k_bias_rows", [P, 2, SEQ], f32r, area_a + 28 * K)
    qk_t = at("qk_t", [P, 2, SEQ], f32, area_a + 32 * K)
    v_parts = at("v_parts", [P, 2, SB, 2, 2, HEAD_DIM], f32r, area_a + 36 * K)
    sb_t = at("sb_t", [P, FLAT], f32, area_a + 44 * K)
    sb_lo = at("sb_lo", [P, FLAT], f32r, area_a + 44 * K)
    sb_hi = at("sb_hi", [P, FLAT], f32r, area_a + 49 * K)
    o_low = [at("sb_o_low", [P, SEQ], f32, area_a + 44 * K), at("fx_o_low", [P, SEQ], f32, area_a + 54 * K)]
    o_sum = [at("sb_o_sum", [P, SEQ], f32, area_a + 46 * K), at("fx_o_sum", [P, SEQ], f32, area_a + 56 * K)]
    fx_p = at("fx_p", [P, FLAT], f32, area_a + 54 * K)
    fx_hi = at("fx_hi", [P, FLAT], f32r, area_a + 54 * K)
    fx_lo = at("fx_lo", [P, FLAT], f32r, area_a + 59 * K)
    later = at("later", [P, LATER], f32, area_a + 59 * K)
    later_lo = at("later_lo", [P, LATER], f32r, area_a + 59 * K)
    later_hi = at("later_hi", [P, LATER], f32r, area_a + 59 * K + 4 * LATER)
    vb_row = at("vb_row", [P, 1024], f32, area_a + 44 * K)
    sq_raw = at("sq_raw", [P, 5, P], f32, area_a + 54 * K)
    wout_hi = at("wout_hi", [P, KB, D_MODEL], f32r, area_a)
    wout_raw = at("wout_raw", [P, KB, D_MODEL], f32, area_a + 32 * K)
    wout_lo = at("wout_lo", [P, KB, D_MODEL], f32r, area_a + 32 * K)
    mg_t = at("mg_t", [P, 2, SEQ], f32, area_a + 64 * K)
    aT = at("aT", [P, FB, SEQ], f32, area_a)
    conv = at("conv", [P, 2, SEQ], f32, area_a + 44 * K)
    gelu = at("gelu", [P, 2, SEQ], f32, area_a + 48 * K)
    q_stack = at("q_stack", [P, SEQ], f32r, area_c + 5952)
    k_stack = at("k_stack", [P, SEQ], f32r, area_c + 5952 + 2 * K)
    f_lhs = at("f_lhs", [P, SEQ], f32, area_c)
    col = at("col", [P, N_COLS], f32, area_c + 2048)
    ident = at("ident", [P, P], f32, area_c + 2048 + 576)
    neg_tri = at("neg_tri", [P, P], f32r, area_c + 2624 + 512)
    neg_one = at("neg_one", [P, P], f32r, area_c + 2624 + 1024)
    ident_bf = at("ident_bf", [P, P], bf16, area_c + 2624 + 1536)
    mask_bf = at("mask_bf", [P, 2, 2, P], bf16, area_c + 2624 + 1792)
    small = area_c + 2624 + 2816
    q_bias = at("q_bias", [P, 4 * PAIRS], f32, small)
    fx_nmax = at("fx_nmax", [P, SB], f32, small + 64)
    fx_sum = at("fx_sum", [P, SB], f32, small + 96)
    fx_rec = at("fx_rec", [P, SB], f32, small + 128)
    bn_parts = at("bn_parts", [P, 2, 6], f32, small + 160)
    bn_mv = at("bn_mv", [P, 2], f32, small + 224)
    ln_var = at("ln_var", [P, 1], f32, small + 256)
    ln_eps = at("ln_eps", [P, 1], f32, small + 416)
    ln_log = at("ln_log", [P, 1], f32, small + 288)
    ln_r0 = at("ln_r0", [P, 1], f32, small + 320)
    ln_nt = at("ln_nt", [P, 1], f32, small + 352)
    ln_r = at("ln_r", [P, 1], f32, small + 384)
    assert COL_MASK + N_FORGET == N_COLS and 4 * N_COLS <= 576

    def plain(ap):
        return ap.bitcast(f32)

    with ExitStack() as ctx:
        ps = ctx.enter_context(nc.psum_tensor("ps", [P, 8 * 512], f32))

        def bank(i):
            return ps[:, 512 * i:512 * (i + 1)]

        SB_PS, FX_PS = 0, 3 * 512

        def sem(name):
            return ctx.enter_context(nc.semaphore(name))

        raw_in = [sem(f"raw_in{i}") for i in range(W_SLOTS)]
        x_in = [sem(f"x_in{k}") for k in range(KB)]
        first_in = sem("first_in")
        const_in, vb_in = sem("const_in"), sem("vb_in")
        row_in = [sem(f"row_in{r}") for r in range(4)]
        wout_in = [sem(f"wout_in{k}") for k in range(KB)]
        last_in = [sem(f"last_in{k}") for k in range(RESIDENT)]
        tok_in = [sem(f"tok_in{s}") for s in range(SB)]
        stored = sem("stored")
        first_hi = sem("first_hi")
        hi_ready, lo_ready = sem("hi_ready"), sem("lo_ready")
        wout_hi_done, wout_split = sem("wout_hi_done"), sem("wout_split")
        block_done = sem("block_done")
        xhi_ready, xlo_ready = sem("xhi_ready"), sem("xlo_ready")
        const_ready = sem("const_ready")
        v_summed = sem("v_summed")
        v_ready = sem("v_ready")
        f_absed, f_exped, f_lned = sem("f_absed"), sem("f_exped"), sem("f_lned")
        f_mined, f_logged, f_cumed = sem("f_mined"), sem("f_logged"), sem("f_cumed")
        f_split, f_lo_done, f_part, f_ready = sem("f_split"), sem("f_lo_done"), sem("f_part"), sem("f_ready")
        block_read = sem("block_read")
        qk_hi_done, qk_split = sem("qk_hi_done"), sem("qk_split")
        v_hi_done, v_split = sem("v_hi_done"), sem("v_split")
        sel_ready = sem("sel_ready")
        sb_scored, sb_summed, sb_mixed = sem("sb_scored"), sem("sb_summed"), sem("sb_mixed")
        sb_absed, sb_exped, sb_lned, sb_weighed = (sem("sb_absed"), sem("sb_exped"), sem("sb_lned"),
                                                   sem("sb_weighed"))
        sb_soft, sb_soft_hi, sb_soft_split = sem("sb_soft"), sem("sb_soft_hi"), sem("sb_soft_split")
        later_part, later_summed = sem("later_part"), sem("later_summed")
        later_hi_done, later_split = sem("later_hi_done"), sem("later_split")
        sb_w_hi, sb_w_split = sem("sb_w_hi"), sem("sb_w_split")
        fx_scored, fx_turned, fx_mixed = sem("fx_scored"), sem("fx_turned"), sem("fx_mixed")
        fx_maxed, fx_exped, fx_inverted, fx_normed = (sem("fx_maxed"), sem("fx_exped"), sem("fx_inverted"),
                                                      sem("fx_normed"))
        fx_w_hi, fx_w_split = sem("fx_w_hi"), sem("fx_w_split")
        o_low_done, o_added = [sem("sb_o_low"), sem("fx_o_low")], [sem("sb_o_added"), sem("fx_o_added")]
        o_hi_done, o_split = [sem("sb_o_hi"), sem("fx_o_hi")], [sem("sb_o_split"), sem("fx_o_split")]
        stack_in = sem("stack_in")
        gated = sem("gated")
        mg_a, mg_b, mg_sum, mg_hi, merged = sem("mg_a"), sem("mg_b"), sem("mg_sum"), sem("mg_hi"), sem("merged")
        out_done = sem("out_done")
        ln_added, ln_stated, ln_aggred, ln_vared = sem("ln_added"), sem("ln_stated"), sem("ln_aggred"), sem("ln_vared")
        ln_logged, ln_rooted, ln_newton, ln_halved, ln_scale = (sem("ln_logged"), sem("ln_rooted"), sem("ln_newton"),
                                                                sem("ln_halved"), sem("ln_scale"))
        ln_gained, ln_done = sem("ln_gained"), sem("ln_done")
        x1_turned, x1_hi_done, x1_split = sem("x1_turned"), sem("x1_hi_done"), sem("x1_split")
        cv_biased, cv_one, cv_done, gelu_done = sem("cv_biased"), sem("cv_one"), sem("cv_done"), sem("gelu_done")
        act_ready, a_hi_done, a_split = sem("act_ready"), sem("a_hi_done"), sem("a_split")

        STACK = 4 * 16
        N_RESIDENT = N_BLOCKS - RESIDENT
        FREE = 1
        FREE_MERGE = 4
        FREE_ACT = 2

        block = ctx.enter_context(nc.Block())

        def rows_of(e):
            return slice(HEAD_DIM * e, HEAD_DIM * (e + 1))

        def other_rows(e):
            return rows_of(1 - e)

        def v_of_pair(pair, b):
            return v_all[:, :, ds(pair * P + D_SB * b, P)].rearrange("p s (e d) -> p s e d", e=2)

        def a_slot(f):
            return f % W_SLOTS if f < FB - 1 else W_SLOTS

        @block.sync
        def _(sp):
            def load(n, slot):
                sp.dma_start(w_raw[:, slot, :], w_stream[ds(n, 1), :, :].rearrange("o p c -> p (o c)")
                             if not isinstance(n, int) else w_stream[n, :, :]).then_inc(raw_in[slot], 16)

            def load_x(k):
                sp.dma_start(xT_raw[:, k, :], xT[k, :, :]).then_inc(x_in[k], 16)

            sp.dma_start(xT_raw[:, 0, :], xT[0, :, :]).then_inc(x_in[0], 16)
            sp.dma_start(w_raw[:, 0, 0:512], w_stream[0, :, 0:512]).then_inc(first_in, 16)
            sp.dma_start(w_raw[:, 0, 512:1024], w_stream[0, :, 512:1024]).then_inc(raw_in[0], 16)
            for k in range(1, W_SLOTS):
                load_x(k)
                load(k, k)
            for k in range(W_SLOTS, KB):
                load_x(k)
            sp.dma_start(col[:], cols).then_inc(const_in, 16)
            sp.dma_start(ident[:], square[:, 0, :]).then_inc(const_in, 16)
            sp.dma_start(sq_raw[:], square).then_inc(const_in, 16)
            sp.dma_start(vb_row[:], rows[0, :].partition_broadcast(P)).then_inc(vb_in, 16)
            def load_row(r):
                sp.dma_start(ln_rows[:, r, :], rows[1 + r, :].partition_broadcast(P)).then_inc(row_in[r], 16)

            def load_when_free(n):
                sp.wait_ge(block_done, n - (W_SLOTS - 1))
                load(n, n % W_SLOTS)

            def stack(e, b):
                src = slice(HEAD_DIM * e, HEAD_DIM * (e + 1))
                k_hi, k_lo = ((qk_hi, 1), (qk_lo, 1)) if b == 0 else ((k_bias_rows, e), (qk_lo, 2))
                for dst, (part, j), low in ((q_stack, (qk_hi, 2 * b), 0), (q_stack, (qk_hi, 2 * b), 1),
                                            (k_stack, k_hi, 0), (k_stack, k_lo, 1)):
                    rows_ = slice(HEAD_DIM * low, HEAD_DIM * (low + 1))
                    sp.dma_start(plain(dst[rows_, :]), plain(part[src, j, :])).then_inc(stack_in, 16)

            for n in range(W_SLOTS, N_PAIR + 3):
                load_when_free(n)
                if n == N_PAIR + 1:
                    sp.wait_ge(qk_split, 2)
                    stack(0, 0)

            def half(pair, e, turn, first):
                h = pair * 2 + e
                for k in range(4):
                    m = first + 3 + k
                    sp.wait_ge(block_done, turn + (m - 3))
                    load(turn + m, m % 4)
                    if k == 0:
                        sp.wait_ge(sb_scored, h + 1)
                        sp.wait_ge(qk_split, pair * 4 + 4)
                        stack(e, 1)
                sp.wait_ge(fx_scored, h + FREE + 1)
                if e == 1:
                    sp.wait_ge(qk_split, (pair + 1) * 4 + 2)
                stack(1 - e, 0)

            with sp.Fori(0, PAIRS - 1) as pair:
                for e in range(2):
                    half(pair, e, pair * 8, N_PAIR + 4 * e)
            load_when_free(N_LAST + 3)
            sp.wait_ge(sb_scored, HALVES - 1)
            stack(1, 0)
            for n in range(N_LAST + 4, N_LAST + 7):
                load_when_free(n)
            load_when_free(N_MERGE + 3)
            sp.wait_ge(fx_mixed, HALVES + FREE)
            for k in range(KB):
                if k == 3:
                    sp.wait_ge(o_split[0], HALVES + FREE)
                    sp.wait_ge(o_split[1], HALVES + FREE)
                sp.dma_start(wout_raw[:, k, :], w_out[P * k:P * (k + 1), :]).then_inc(wout_in[k], 16)
                if k % 2 == 1:
                    load_when_free(N_MERGE + 4 + k // 2)
            for s in range(SB):
                load_when_free(N_UP + s)
                sp.wait_ge(merged, FREE_MERGE + 2 * s + 2)
                sp.dma_start(x1[:, s, :], x_tok[P * s:P * (s + 1), :]).then_inc(tok_in[s], 16)
                if s < 2:
                    load_row(s)
            n_loop = (N_DOWN + 3 - N_UP - 4) // 4
            with sp.Fori(0, n_loop) as i:
                for j in range(4):
                    sp.wait_ge(block_done, 4 * i + (N_UP + 1 + j))
                    load(4 * i + (N_UP + 4 + j), (N_UP + j) % 4)
            for n in range(N_UP + 4 + 4 * n_loop, N_DOWN + 4):
                load_when_free(n)
            for r in range(2, 4):
                load_row(r)
            sp.wait_ge(block_done, N_DOWN)
            for k in range(RESIDENT):
                sp.dma_start(r_raw[:, k, :], w_stream[N_RESIDENT + k, :, :]).then_inc(last_in[k], 16)
            n_loop = (N_RESIDENT - N_DOWN - 4) // 4
            with sp.Fori(0, n_loop) as i:
                for j in range(4):
                    sp.wait_ge(block_done, 4 * i + (N_DOWN + 1 + j))
                    load(4 * i + (N_DOWN + 4 + j), (N_DOWN + j) % 4)
            for n in range(N_DOWN + 4 + 4 * n_loop, N_RESIDENT):
                load_when_free(n)
            for s in range(SB):
                for half_ in range(2):
                    cs = slice(512 * half_, 512 * (half_ + 1))
                    sp.wait_ge(ln_done, 2 * (SB + s) + half_ + 1)
                    sp.dma_start(out[P * s:P * (s + 1), cs], x1[:, s, cs]).then_inc(stored, 16)
            sp.wait_ge(stored, 16 * 2 * SB)

        @block.gpsimd
        def _(pool):
            def low(n, slot):
                pool.wait_ge(hi_ready, n + 1)
                nc.gpsimd.tensor_tensor(w_lo[:, slot, :], w_raw[:, slot, :], plain(w_hi[:, slot, :]),
                                        ALU.subtract).then_inc(lo_ready, 1)

            def v_low(pair):
                for b in range(2):
                    pool.wait_ge(v_hi_done, pair * 2 + (b + 1))
                    nc.gpsimd.tensor_tensor(v_parts[:, b, :, :, 1, :], v_of_pair(pair, b),
                                            plain(v_parts[:, b, :, :, 0, :]), ALU.subtract).then_inc(v_split, 1)

            assert (N_PAIR + 3) % 4 == 0
            with pool.Fori(0, (N_PAIR + 3) // 4) as i:
                for j in range(4):
                    low(4 * i + j, j)
            pool.wait_ge(v_ready, 2 * SB)
            with pool.Fori(0, PAIRS - 1) as pair:
                v_low(pair)
                for j in range(8):
                    low(pair * 8 + (N_PAIR + 3 + j), j % 4)
            v_low(PAIRS - 1)
            for n in range(N_LAST + 3, N_MERGE + 1):
                low(n, n % 4)
            with pool.Fori(0, 2) as i:
                for j in range(4):
                    d = 4 * i + j
                    low(4 * i + (N_MERGE + 1 + j), (N_MERGE + 1 + j) % 4)
                    pool.wait_ge(wout_hi_done, d + 1)
                    row_block = (slice(None), ds(d, 1))
                    nc.gpsimd.tensor_tensor(wout_lo[row_block].rearrange("p o c -> p (o c)"),
                                            wout_raw[row_block].rearrange("p o c -> p (o c)"),
                                            plain(wout_hi[row_block].rearrange("p o c -> p (o c)")),
                                            ALU.subtract).then_inc(wout_split, 1)
            n_loop = (N_RESIDENT - N_UP - 1) // 4
            with pool.Fori(0, n_loop) as i:
                for j in range(4):
                    low(4 * i + (N_UP + 1 + j), (N_UP + 1 + j) % 4)
            for n in range(N_UP + 1 + 4 * n_loop, N_RESIDENT):
                low(n, n % 4)
            for k in range(RESIDENT):
                pool.wait_ge(hi_ready, N_RESIDENT + k + 1)
                nc.gpsimd.tensor_tensor(r_lo[:, k, :], r_raw[:, k, :], plain(r_hi[:, k, :]),
                                        ALU.subtract).then_inc(lo_ready, 1)
        @block.scalar
        def _(act):
            def table(index):
                act.add_instruction(mybir.InstLoadActFuncSet(
                    name=nc.get_next_instruction_name(), act_func_set_id=index,
                    engine=mybir.EngineType.Activation))

            def arrived(n, slot, turn):
                act.wait_ge(raw_in[slot], turn * 16 + 16)

            def high(n, slot, turn, used):
                arrived(n, slot, turn)
                if used is not None:
                    act.wait_ge(block_done, used)
                nc.scalar.activation(w_hi[:, slot, :], w_raw[:, slot, :], ACT.Copy).then_inc(hi_ready, 1)

            def high_in_order(n):
                high(n, n % 4, n // 4, n - 3 if n >= 4 else None)

            table(SET_LN_EXP)
            for k in range(KB):
                act.wait_ge(x_in[k], 16)
                nc.scalar.activation(xT_hi[:, k, :], xT_raw[:, k, :], ACT.Copy).then_inc(xhi_ready, 1)
                if k > 0:
                    high_in_order(k)
                    continue
                act.wait_ge(first_in, 16)
                nc.scalar.activation(w_hi[:, 0, 0:512], w_raw[:, 0, 0:512], ACT.Copy).then_inc(first_hi, 1)
                arrived(0, 0, 0)
                nc.scalar.activation(w_hi[:, 0, 512:1024], w_raw[:, 0, 512:1024], ACT.Copy).then_inc(hi_ready, 1)
            for n in range(N_F, N_F + 3):
                high_in_order(n)
            high_in_order(N_F + 3)
            act.wait_ge(block_done, N_F + 1)
            act.wait_ge(const_in, 48)
            nc.scalar.activation(f_e[:], bank(0), ACT.Abs, bias=col[:, COL_F:COL_F + 1]).then_inc(f_absed, 1)
            act.wait_ge(f_absed, 1)
            nc.scalar.activation(f_e[:], f_e[:], ACT.Exp, scale=-1.0).then_inc(f_exped, 1)
            act.wait_ge(f_exped, 1)
            nc.scalar.activation(f_e[:], f_e[:], ACT.Ln, bias=1.0).then_inc(f_lned, 1)

            def read_qk(pair, j, bank_, done, free):
                act.wait_ge(block_done, done)
                if free is not None:
                    act.wait_ge(qk_split, free)
                bias = (q_bias if j % 2 == 0 else col)[:, ds(pair * 4 + j, 1)]
                nc.scalar.activation(qk_t[:, j % 2, :], bank(bank_), ACT.Identity, bias=bias,
                                     scale=HEAD_DIM ** -0.5 if j % 2 == 0 else 1.0).then_inc(block_read, 1)

            act.wait_ge(const_ready, 1)
            for j in range(4):
                high_in_order(N_QK0 + j + 3)
                read_qk(0, j, 6 + j % 2, N_QK0 + j + 1, j - 1 if j >= 2 else None)

            def read_block(pair, place, blocks, n):
                kind, index, bank_ = blocks[place]
                if kind == "gate":
                    act.wait_ge(block_done, n + 1)
                    nc.scalar.activation(g_all[:, ds(index, 1), :].rearrange("p o c -> p (o c)"), bank(bank_),
                                         ACT.Identity, bias=col[:, ds(COL_G + index, 1)]).then_inc(block_read, 1)
                else:
                    read_qk(pair + 1, index, bank_, n + 1, (pair + 1) * 4 + (index - 1))

            def half(pair, e, blocks, n0, highs):
                h = pair * 2 + e
                at_place = {pl: n0 + k for k, pl in enumerate(sorted(blocks))}
                act.wait_ge(o_split[0], h + FREE)
                act.wait_ge(sb_scored, h + 1)
                nc.scalar.activation(sb_t[:], ps[:, SB_PS:SB_PS + FLAT], ACT.Abs).then_inc(sb_absed, 1)
                act.wait_ge(sb_absed, h + 1)
                nc.scalar.activation(sb_t[:], sb_t[:], ACT.Exp, scale=-1.0).then_inc(sb_exped, 1)
                act.wait_ge(sb_exped, h + 1)
                nc.scalar.activation(sb_t[:], sb_t[:], ACT.Ln, bias=1.0).then_inc(sb_lned, 1)
                if e == 0:
                    act.wait_ge(sb_mixed, h + FREE)
                    act.wait_ge(fx_mixed, h + FREE)
                    for b in range(2):
                        nc.scalar.activation(v_parts[:, b, :, :, 0, :], v_of_pair(pair, b),
                                             ACT.Copy).then_inc(v_hi_done, 1)
                if 0 in blocks:
                    highs(0)
                    read_block(pair, 0, blocks, at_place[0])
                act.wait_ge(o_split[1], h + FREE)
                act.wait_ge(fx_maxed, h * SB + SB)
                for r in range(SB):
                    off, width = FX_OFF[r], P * (r + 1)
                    nc.scalar.activation(fx_p[:, off:off + width], ps[:, FX_PS + off:FX_PS + off + width], ACT.Exp,
                                         bias=fx_nmax[:, r:r + 1],
                                         accum_out=fx_sum[:, r:r + 1]).then_inc(fx_exped, 1)
                if 1 in blocks:
                    highs(1)
                    read_block(pair, 1, blocks, at_place[1])
                act.wait_ge(sb_summed, h + 1)
                nc.scalar.activation(sb_t[:], ps[:, SB_PS:SB_PS + FLAT], ACT.Exp).then_inc(sb_weighed, 1)
                if 2 in blocks:
                    highs(2)
                    read_block(pair, 2, blocks, at_place[2])
                act.wait_ge(fx_turned, h + 1)
                nc.scalar.activation(fx_hi[:], ps[:, FX_PS:FX_PS + FLAT], ACT.Copy).then_inc(fx_w_hi, 1)
                if 3 in blocks:
                    highs(3)
                    read_block(pair, 3, blocks, at_place[3])
                for b, mixed in ((0, sb_mixed), (1, fx_mixed)):
                    act.wait_ge(mixed, h + FREE + 1)
                    nc.scalar.activation(o_low[b][HEAD_DIM * e:HEAD_DIM * (e + 1), :],
                                         ps[HEAD_DIM:P, 512 * (6 + b):512 * (7 + b)], ACT.Copy
                                         ).then_inc(o_low_done[b], 1)

            act.wait_ge(v_ready, 2 * SB)
            act.sem_inc(sb_weighed, FREE)
            act.sem_inc(fx_exped, FREE * SB)
            with act.Fori(0, PAIRS - 1) as pair:
                for e in range(2):
                    n0 = pair * 8 + (N_PAIR + 4 * e)

                    def highs(place, n0=n0, e=e):
                        m = N_PAIR + 4 * e + place + 3
                        high(None, m % 4, pair * 2 + m // 4, pair * 8 + (m - 3))
                    half(pair, e, loop_blocks(pair)[e], n0, highs)
            for e in range(2):
                def highs(place, e=e):
                    n = N_LAST + 2 * e + (place // 2) + 3
                    high_in_order(n)
                half(PAIRS - 1, e, LAST_BLOCKS[e], N_LAST + 2 * e, highs)

            table(SET_SIGMOID)
            act.wait_ge(sb_mixed, HALVES + FREE)
            act.wait_ge(fx_mixed, HALVES + FREE)
            for d in range(KB):
                for b in range(2):
                    gate = g_all[:, d + KB * b, :]
                    nc.scalar.activation(gate, gate, ACT.Sigmoid).then_inc(gated, 1)
                high_in_order(N_MERGE + d + 3)
                act.wait_ge(wout_in[d], 16)
                nc.scalar.activation(wout_hi[:, d, :], wout_raw[:, d, :], ACT.Copy).then_inc(wout_hi_done, 1)

            def root(k):
                act.wait_ge(ln_aggred, k + 1)
                nc.scalar.activation(ln_log[:], bn_mv[:, 1:2], ACT.Ln, bias=ln_eps[:]).then_inc(ln_logged, 1)
                act.wait_ge(ln_logged, k + 1)
                nc.scalar.activation(ln_r0[:], ln_log[:], ACT.Exp, scale=-0.5).then_inc(ln_rooted, 1)

            table(SET_LN_EXP)

            def x1_high(s):
                for half_ in range(2):
                    act.wait_ge(x1_turned, 2 * s + half_ + 1)
                    nc.scalar.activation(x1T_hi[:, 4 * half_:4 * half_ + 4, P * s:P * (s + 1)],
                                         bank(2 * s + half_).rearrange("p (k c) -> p k c", c=P),
                                         ACT.Copy).then_inc(x1_hi_done, 1)

            for s in range(SB):
                if s > 0:
                    x1_high(s - 1)
                root(s)
            x1_high(SB - 1)

            table(SET_GELU)

            def a_high(f, slot):
                act.wait_ge(act_ready, f + (FREE_ACT + 1))
                if not isinstance(f, int) or W_SLOTS <= f < FB - 1:
                    act.wait_ge(block_done, f + (N_DOWN - W_SLOTS + 1))
                nc.scalar.activation(a_hi[:, slot, :], aT[:, ds(f, 1), :].rearrange("p o c -> p (o c)"),
                                     ACT.Copy).then_inc(a_hi_done, 1)

            def up_pair(i):
                for j in range(2):
                    f = 2 * i + j
                    for g in range(2):
                        m = N_UP + 2 * j + g + 3
                        high(None, m % 4, i + m // 4, 4 * i + (m - 3))
                    act.wait_ge(block_done, 4 * i + (N_UP + 2 * j + 1))
                    act.wait_ge(act_ready, f + 1)
                    nc.scalar.activation(conv[:, j, :], bank(2 * j), ACT.Identity,
                                         bias=col[:, ds(COL_CB + f, 1)],
                                         scale=col[:, ds(f * CONV_WIDTH + (COL_CW + CONV_WIDTH - 1), 1)]
                                         ).then_inc(cv_biased, 1)
                    act.wait_ge(cv_done, f + 1)
                    nc.scalar.activation(gelu[:, j, :], conv[:, j, :], ACT.Gelu).then_inc(gelu_done, 1)

            with act.Fori(0, FB // 2 - 1) as i:
                up_pair(i)
            a_high(0, 0)
            a_high(1, 1)
            up_pair(FB // 2 - 1)

            table(SET_LN_EXP)
            for f in range(2):
                a_high(f + 2, f + 2)
                high_in_order(N_DOWN + f + 3)
            n_loop = (N_RESIDENT - N_DOWN - 5) // 4
            with act.Fori(0, n_loop) as i:
                for j in range(4):
                    a_high(4 * i + (j + 4), j)
                    m = N_DOWN + 2 + j + 3
                    high(None, m % 4, i + m // 4, 4 * i + (m - 3))
            assert N_DOWN + 4 * n_loop + 5 == N_RESIDENT
            for k in range(RESIDENT):
                act.wait_ge(last_in[k], 16)
                nc.scalar.activation(r_hi[:, k, :], r_raw[:, k, :], ACT.Copy).then_inc(hi_ready, 1)
            for f in range(4 + 4 * n_loop, FB):
                a_high(f, a_slot(f))
            for s in range(SB):
                root(SB + s)

        @block.vector
        def _(dve):
            def split_lo(out_lo, whole, part_hi):
                return nc.vector.tensor_tensor(out_lo, whole, plain(part_hi), ALU.subtract)

            for k in range(KB):
                dve.wait_ge(xhi_ready, k + 1)
                split_lo(xT_lo[:, k, :], xT_raw[:, k, :], xT_hi[:, k, :]).then_inc(xlo_ready, 1)
            dve.wait_ge(const_in, 48)
            nc.vector.tensor_scalar(q_bias[:], col[:, COL_QK:COL_QK + 4 * PAIRS], HEAD_DIM ** -0.5, None,
                                    ALU.mult)
            nc.vector.tensor_copy(neg_tri[:], sq_raw[:, 1, :])
            nc.vector.tensor_copy(neg_one[:], sq_raw[:, 2, :])
            nc.vector.tensor_copy(ident_bf[:], sq_raw[:, 0, :])
            for side in range(2):
                nc.vector.tensor_copy(mask_bf[:, :, side, :], sq_raw[:, 3:5, :])
            nc.vector.memset(ln_eps[:], LN_EPS)
            nc.vector.memset(f_zero[:], 0.0).then_inc(const_ready, 1)
            dve.wait_ge(vb_in, 16)
            for i, b in enumerate(V_READ):
                s, br = b // 2, b % 2
                if i < 2 * SB - 1:
                    dve.wait_ge(v_summed, i + 1)
                else:
                    dve.wait_ge(block_done, KB)
                nc.vector.tensor_tensor(v_all[:, s, 512 * br:512 * (br + 1)], bank(b),
                                        vb_row[:, 512 * br:512 * (br + 1)], ALU.add).then_inc(v_ready, 1)

            dve.wait_ge(block_done, N_F + 1)
            dve.wait_ge(f_absed, 1)
            nc.vector.tensor_scalar(f_min[:], bank(0), col[:, COL_F:COL_F + 1], 0.0, ALU.add,
                                    ALU.min).then_inc(f_mined, 1)
            dve.wait_ge(f_mined, 1)
            dve.wait_ge(f_lned, 1)
            nc.vector.tensor_tensor(f_log[:], f_min[:], f_e[:], ALU.subtract).then_inc(f_logged, 1)
            dve.wait_ge(f_logged, 1)
            nc.vector.tensor_tensor_scan(f_cum[:], f_log[:], f_zero[:], 0.0, ALU.add, ALU.add).then_inc(f_cumed, 1)
            dve.wait_ge(f_cumed, 1)
            nc.vector.tensor_copy(f_hi[:], f_cum[:]).then_inc(f_split, 1)
            dve.wait_ge(f_split, 1)
            split_lo(f_lo[:], f_cum[:], f_hi[:]).then_inc(f_lo_done, 1)
            dve.wait_ge(f_lo_done, 1)
            for k, (c0, sides) in enumerate(((COL_SEL, [(k_bias_rows[other_rows(e), e, :], other_rows(e))
                                                        for e in range(2)]),
                                             (COL_SEL + 3, [(f_lhs[:], slice(0, P))]))):
                if k:
                    dve.wait_ge(f_ready, 2)
                nc.vector.tensor_scalar(f_tmp[:], plain(f_lo[:]), col[:, c0 + 1:c0 + 2], col[:, c0 + 2:c0 + 3],
                                        ALU.mult, ALU.add).then_inc(f_part, 1)
                dve.wait_ge(f_part, k + 1)
                for side, r in sides:
                    nc.vector.scalar_tensor_tensor(side, plain(f_hi[r, :]), col[r, c0:c0 + 1], f_tmp[r, :],
                                                   ALU.mult, ALU.add).then_inc(f_ready, 1)
            dve.wait_ge(f_ready, 3)

            def select_bias(h, e):
                other = other_rows(e)
                nc.vector.tensor_scalar(q_bias_rows[other, e, :], f_lhs[other, :], col[other, ds(COL_MASK + h, 1)],
                                        None, ALU.mult).then_inc(sel_ready, 1)

            def split_qk(j, m, read):
                dve.wait_ge(block_read, read)
                whole = qk_t[:, j % 2, :]
                halves = [(rows_of(e), e) for e in range(2)]
                if j == 3:
                    for r, e in halves:
                        hi = nc.vector.tensor_copy(k_bias_rows[r, e, :], qk_t[r, 1, :])
                else:
                    hi = nc.vector.tensor_copy(qk_hi[:, j, :], whole)
                hi.then_inc(qk_hi_done, 1)
                dve.wait_ge(qk_hi_done, m + 1)
                if j < 2:
                    lo = split_lo(qk_lo[:, j, :], whole, qk_hi[:, j, :])
                elif j == 2:
                    for r, e in halves:
                        lo = split_lo(q_bias_rows[r, e, :], qk_t[r, 0, :], qk_hi[r, 2, :])
                else:
                    for r, e in halves:
                        lo = split_lo(qk_lo[r, 2, :], qk_t[r, 1, :], k_bias_rows[r, e, :])
                lo.then_inc(qk_split, 1)

            select_bias(0, 0)
            for j in range(4):
                split_qk(j, j, j + 1)

            def split_next(pair, j):
                if j < 2:
                    dve.wait_ge(sb_scored, pair * 2 + 2)
                else:
                    dve.wait_ge(fx_scored, pair * 2 + (2 + FREE))
                split_qk(j, pair * 4 + (4 + j), pair * 8 + (4 + 4 + j + 1))

            def fx_max(h):
                dve.wait_ge(fx_scored, h + FREE + 1)
                dve.wait_ge(fx_exped, h * SB + FREE * SB)
                for r in range(SB):
                    off, width = FX_OFF[r], P * (r + 1)
                    nc.vector.tensor_reduce(fx_nmax[:, r:r + 1], ps[:, FX_PS + off:FX_PS + off + width], AX.X,
                                            ALU.max, negate=True).then_inc(fx_maxed, 1)

            def half(pair, e, qk):
                h = pair * 2 + e
                last = isinstance(pair, int)
                if last:
                    fx_max(h)
                    if e == 0:
                        select_bias(h + 1, 1)
                dve.wait_ge(sb_lned, h + 1)
                nc.vector.scalar_tensor_tensor(sb_t[:], ps[:, SB_PS:SB_PS + FLAT], 0.0, sb_t[:], ALU.max,
                                               ALU.add).then_inc(sb_soft, 1)
                dve.wait_ge(sb_soft, h + 1)
                nc.vector.tensor_copy(sb_hi[:], sb_t[:]).then_inc(sb_soft_hi, 1)
                nc.vector.tensor_tensor(later[:, LATER_OFF[1] + P:LATER_OFF[1] + 2 * P],
                                        sb_t[:, SB_OFF[2] + P:SB_OFF[2] + 2 * P], sb_t[:, SB_OFF[3]:SB_OFF[3] + P],
                                        ALU.add).then_inc(later_part, 1)
                nc.vector.tensor_copy(later[:, LATER_OFF[1]:LATER_OFF[1] + P],
                                      sb_t[:, SB_OFF[2]:SB_OFF[2] + P]).then_inc(later_part, 1)
                nc.vector.tensor_copy(later[:, 0:P], sb_t[:, SB_OFF[1]:SB_OFF[1] + P]).then_inc(later_part, 1)
                dve.wait_ge(later_part, h * 3 + 3)
                nc.vector.tensor_tensor(later[:, P:3 * P], sb_t[:, SB_OFF[1] + P:SB_OFF[1] + 3 * P],
                                        later[:, LATER_OFF[1]:LATER_OFF[1] + 2 * P],
                                        ALU.add).then_inc(later_summed, 1)
                dve.wait_ge(sb_soft_hi, h + 1)
                dve.wait_ge(later_summed, h + 1)
                split_lo(sb_lo[:], sb_t[:], sb_hi[:]).then_inc(sb_soft_split, 1)
                nc.vector.tensor_copy(later_hi[:], later[:]).then_inc(later_hi_done, 1)
                dve.wait_ge(later_hi_done, h + 1)
                split_lo(later_lo[:], later[:], later_hi[:]).then_inc(later_split, 1)
                if not last:
                    fx_max(h)
                    select_bias(h + 1, 1 - e)
                if qk:
                    split_next(pair, 0)
                dve.wait_ge(fx_exped, h * SB + (FREE + 1) * SB)
                dve.wait_ge(fx_normed, h * SB + FREE * SB)
                nc.vector.reciprocal(fx_rec[:], fx_sum[:]).then_inc(fx_inverted, 1)
                dve.wait_ge(fx_inverted, h + 1)
                for r in range(SB):
                    off, width = FX_OFF[r], P * (r + 1)
                    nc.vector.tensor_scalar(fx_p[:, off:off + width], fx_p[:, off:off + width],
                                            fx_rec[:, r:r + 1], None, ALU.mult).then_inc(fx_normed, 1)
                if qk:
                    split_next(pair, 1)
                dve.wait_ge(sb_weighed, h + FREE + 1)
                nc.vector.tensor_copy(sb_hi[:], sb_t[:]).then_inc(sb_w_hi, 1)
                dve.wait_ge(sb_w_hi, h + 1)
                split_lo(sb_lo[:], sb_t[:], sb_hi[:]).then_inc(sb_w_split, 1)
                if qk:
                    split_next(pair, 2)
                dve.wait_ge(fx_w_hi, h + 1)
                split_lo(fx_lo[:], ps[:, FX_PS:FX_PS + FLAT], fx_hi[:]).then_inc(fx_w_split, 1)
                if qk:
                    split_next(pair, 3)
                rows_ = slice(HEAD_DIM * e, HEAD_DIM * (e + 1))
                for b in range(2):
                    where = (rows_, ds(pair + PAIRS * b, 1))
                    o_hi = oT_hi[where].rearrange("p o c -> p (o c)")
                    dve.wait_ge(o_low_done[b], h + 1)
                    nc.vector.tensor_tensor(o_sum[b][rows_, :], ps[0:HEAD_DIM, 512 * (6 + b):512 * (7 + b)],
                                            o_low[b][rows_, :], ALU.add).then_inc(o_added[b], 1)
                    dve.wait_ge(o_added[b], h + FREE + 1)
                    nc.vector.tensor_copy(o_hi, o_sum[b][rows_, :]).then_inc(o_hi_done[b], 1)
                    dve.wait_ge(o_hi_done[b], h + 1)
                    split_lo(oT_lo[where].rearrange("p o c -> p (o c)"), o_sum[b][rows_, :],
                             o_hi).then_inc(o_split[b], 1)

            dve.sem_inc(fx_normed, FREE * SB)
            dve.sem_inc(fx_w_split, FREE)
            dve.sem_inc(o_split[0], FREE)
            dve.sem_inc(o_split[1], FREE)
            dve.sem_inc(o_added[0], FREE)
            dve.sem_inc(o_added[1], FREE)
            dve.sem_inc(merged, FREE_MERGE)
            with dve.Fori(0, PAIRS - 1) as pair:
                for e in range(2):
                    half(pair, e, e == 1)
            for e in range(2):
                half(PAIRS - 1, e, False)

            with dve.Fori(0, 2) as i:
                for j in range(4):
                    d = 4 * i + j
                    dve.wait_ge(block_done, d + (N_MERGE + 1))
                    dve.wait_ge(gated, d * 2 + 2)
                    dve.wait_ge(merged, d + FREE_MERGE)
                    for b, done in ((0, mg_a), (1, mg_b)):
                        nc.vector.tensor_tensor(mg_t[:, b, :], bank(MERGE_BANKS[j] + b),
                                                g_all[:, ds(d + KB * b, 1), :].rearrange("p o c -> p (o c)"),
                                                ALU.mult).then_inc(done, 1)
                    dve.wait_ge(mg_a, d + 1)
                    dve.wait_ge(mg_b, d + 1)
                    nc.vector.tensor_tensor(mg_t[:, 0, :], mg_t[:, 0, :], mg_t[:, 1, :], ALU.add).then_inc(mg_sum, 1)
                    dve.wait_ge(mg_sum, d + 1)
                    m_hi = mT_hi[:, ds(d, 1), :].rearrange("p o c -> p (o c)")
                    nc.vector.tensor_copy(m_hi, mg_t[:, 0, :]).then_inc(mg_hi, 1)
                    dve.wait_ge(mg_hi, d + 1)
                    split_lo(mT_lo[:, ds(d, 1), :].rearrange("p o c -> p (o c)"), mg_t[:, 0, :],
                             m_hi).then_inc(merged, 1)

            def half_of(s, half_):
                return x1[:, s, 512 * half_:512 * (half_ + 1)]

            def ln_add(s, k, half_, bank_):
                part = half_of(s, half_)
                dve.wait_ge(out_done, 2 * k + half_ + 1)
                nc.vector.scalar_tensor_tensor(part, part, ALPHA, bank(bank_), ALU.mult,
                                               ALU.add).then_inc(ln_added, 1)
                dve.wait_ge(ln_added, 2 * k + half_ + 1)
                nc.vector.bn_stats(bn_parts[:, half_, :], part).then_inc(ln_stated, 1)

            def ln_norm(s, k, gain):
                dve.wait_ge(ln_stated, 2 * k + 2)
                nc.vector.bn_aggr(bn_mv[:], bn_parts[:].rearrange("p a b -> p (a b)")).then_inc(ln_aggred, 1)
                dve.wait_ge(ln_aggred, k + 1)
                nc.vector.tensor_scalar(ln_var[:], bn_mv[:, 1:2], LN_EPS, None, ALU.add).then_inc(ln_vared, 1)
                if s == 0:
                    dve.wait_ge(row_in[gain], 16)
                nc.vector.scalar_tensor_tensor(x1[:, s, :], x1[:, s, :], bn_mv[:, 0:1], ln_rows[:, gain, :],
                                               ALU.subtract, ALU.mult).then_inc(ln_gained, 1)
                dve.wait_ge(ln_vared, k + 1)
                dve.wait_ge(ln_rooted, k + 1)
                nc.vector.scalar_tensor_tensor(ln_nt[:], ln_r0[:], ln_r0[:], ln_var[:], ALU.mult,
                                               ALU.mult).then_inc(ln_newton, 1)
                dve.wait_ge(ln_newton, k + 1)
                nc.vector.tensor_scalar(ln_nt[:], ln_nt[:], -0.5, 1.5, ALU.mult, ALU.add).then_inc(ln_halved, 1)
                dve.wait_ge(ln_halved, k + 1)
                nc.vector.tensor_tensor(ln_r[:], ln_nt[:], ln_r0[:], ALU.mult).then_inc(ln_scale, 1)
                dve.wait_ge(ln_scale, k + 1)
                dve.wait_ge(ln_gained, k + 1)
                if s == 0:
                    dve.wait_ge(row_in[gain + 1], 16)
                for half_ in range(2):
                    part = half_of(s, half_)
                    nc.vector.scalar_tensor_tensor(part, part, ln_r[:],
                                                   ln_rows[:, gain + 1, 512 * half_:512 * (half_ + 1)],
                                                   ALU.mult, ALU.add).then_inc(ln_done, 1)

            def x1_low(s):
                for half_ in range(2):
                    dve.wait_ge(x1_hi_done, 2 * s + half_ + 1)
                    where = (slice(None), slice(4 * half_, 4 * half_ + 4), slice(P * s, P * (s + 1)))
                    split_lo(x1T_lo[where], bank(2 * s + half_).rearrange("p (k c) -> p k c", c=P),
                             x1T_hi[where]).then_inc(x1_split, 1)

            for s in range(SB):
                dve.wait_ge(tok_in[s], 16)
                ln_add(s, s, 0, 2 * s)
                if s > 0:
                    x1_low(s - 1)
                ln_add(s, s, 1, 2 * s + 1)
                ln_norm(s, s, 0)
            x1_low(SB - 1)
            dve.wait_ge(x1_split, 2 * SB - 2)
            dve.sem_inc(act_ready, FREE_ACT)

            def up_pair(i):
                for j in range(2):
                    f = 2 * i + j
                    for t, (before, after) in ((1, (cv_biased, cv_one)), (2, (cv_one, cv_done))):
                        dve.wait_ge(before, f + 1)
                        nc.vector.scalar_tensor_tensor(
                            conv[:, j, t:SEQ], ps[:, 512 * 2 * j:512 * (2 * j + 1) - t],
                            col[:, ds(f * CONV_WIDTH + (COL_CW + CONV_WIDTH - 1 - t), 1)], conv[:, j, t:SEQ],
                            ALU.mult, ALU.add).then_inc(after, 1)
                    dve.wait_ge(gelu_done, f + 1)
                    dve.wait_ge(block_done, 4 * i + (N_UP + 2 * j + 2))
                    nc.vector.tensor_tensor(aT[:, ds(f, 1), :].rearrange("p o c -> p (o c)"), bank(2 * j + 1),
                                            gelu[:, j, :], ALU.mult).then_inc(act_ready, 1)

            def a_low(f, slot):
                dve.wait_ge(a_hi_done, f + 1)
                split_lo(a_lo[:, slot, :], aT[:, ds(f, 1), :].rearrange("p o c -> p (o c)"),
                         a_hi[:, slot, :]).then_inc(a_split, 1)

            with dve.Fori(0, FB // 2 - 1) as i:
                up_pair(i)
            a_low(0, 0)
            a_low(1, 1)
            up_pair(FB // 2 - 1)

            n_loop = (FB - 3) // 4
            with dve.Fori(0, n_loop) as i:
                for j in range(4):
                    a_low(4 * i + (j + 2), (j + 2) % 4)
            for f in range(2 + 4 * n_loop, FB):
                a_low(f, a_slot(f))
            for s in range(SB):
                for half_ in range(2):
                    ln_add(s, SB + s, half_, DOWN_BANKS[s][half_])
                ln_norm(s, SB + s, 2)

        @block.tensor
        def _(pe):
            def product(out_, lhs, rhs, start=False, stop=False):
                return nc.tensor.matmul(out_, lhs, rhs, start=start, stop=stop, skip_group_check=True)

            def split_product(out_, l_hi, l_lo, r_hi, r_lo, start, stop):
                product(out_, l_hi, r_hi, start=start)
                product(out_, l_hi, r_lo)
                return product(out_, l_lo, r_hi, stop=stop)

            def weight_ready(n):
                pe.wait_ge(lo_ready, n + 1)

            def column_block(n, slot, bank_, ks=range(KB)):
                weight_ready(n)
                for k in ks:
                    w = (slice(None), slot, slice(P * k, P * (k + 1)))
                    last = split_product(bank(bank_), w_hi[w], w_lo[w], xT_hi[:, k, :], xT_lo[:, k, :],
                                         k == 0, k == KB - 1)
                if KB - 1 in ks:
                    last.then_inc(block_done, 1)

            def v_product(b, k, x_part, w_part, start=False, stop=False):
                s, br = b // 2, b % 2
                return product(bank(b), x_part[:, k, P * s:P * (s + 1)],
                               w_part[:, k % W_SLOTS, 512 * br:512 * (br + 1)], start=start, stop=stop)

            for k in range(KB - 1):
                for turn_, (ready_x, x_part, ready_w, w_part) in enumerate((
                        (xhi_ready, xT_hi, hi_ready, w_hi), (xlo_ready, xT_lo, hi_ready, w_hi),
                        (xlo_ready, xT_hi, lo_ready, w_lo))):
                    pe.wait_ge(ready_x, k + 1)
                    if k == 0 and turn_ == 0:
                        pe.wait_ge(first_hi, 1)
                    else:
                        pe.wait_ge(ready_w, k + 1)
                    for b in (0, 2, 4, 6, 1, 3, 5, 7):
                        if k == 0 and turn_ == 0 and b == 1:
                            pe.wait_ge(hi_ready, 1)
                        last = v_product(b, k, x_part, w_part, start=k == 0 and turn_ == 0)
                last.then_inc(block_done, 1)
            pe.wait_ge(xlo_ready, KB)
            weight_ready(KB - 1)
            for b in V_READ:
                v_product(b, KB - 1, xT_hi, w_hi)
                v_product(b, KB - 1, xT_lo, w_hi)
                last = v_product(b, KB - 1, xT_hi, w_lo, stop=True)
                last.then_inc(v_summed if b != V_READ[-1] else block_done, 1)
            pe.wait_ge(v_ready, 1)
            column_block(N_F, N_F % 4, 0)
            for j in range(4):
                if j < 2:
                    pe.wait_ge(v_ready, 2 + j)
                else:
                    pe.wait_ge(block_read, j - 1)
                column_block(N_QK0 + j, (N_QK0 + j) % 4, 6 + j % 2)

            def masked(base, places, branch):
                for o, n_blocks in places:
                    mask = mask_bf[:, branch, 0:n_blocks, :].rearrange("p s c -> p (s c)")
                    last = product(ps[:, base + o:base + o + P * n_blocks], ident_bf[:], mask)
                return last

            def half(pair, e, blocks, turn, first):
                h = pair * 2 + e
                n0 = turn + first
                b0 = turn + (first - N_QK0)
                hd = slice(HEAD_DIM * e, HEAD_DIM * (e + 1))
                order = sorted(blocks)

                shares = (KB,) * 4 if len(order) == 4 else LAST_SHARES

                def fill(place):
                    at_, end = sum(shares[:place]), sum(shares[:place + 1])
                    while at_ < end:
                        k, row = at_ // KB, at_ % KB
                        rows_ = range(row, min(KB, row + end - at_))
                        bank_ = blocks[order[k]][2]
                        if row == 0 and k < 2:
                            pe.wait_ge(o_added[bank_ - 6], h + FREE)
                            pe.wait_ge(block_read, 3 + bank_ - 6)
                        elif row == 0:
                            pe.wait_ge(block_read, b0 + (k - 1))
                        column_block(n0 + k, (first + k) % 4, bank_, rows_)
                        at_ += len(rows_)

                pe.wait_ge(qk_split, pair * 4 + 2)
                pe.wait_ge(sb_weighed, h + FREE)
                pe.wait_ge(v_ready, 2 * SB)
                pe.wait_ge(f_mined, 1)
                pe.wait_ge(f_absed, 1)
                last_pair = isinstance(pair, int)
                pe.wait_ge(stack_in, h * (2 * STACK) + STACK if not (last_pair and e == 1) else h * (2 * STACK))
                for r in range(SB):
                    o = SB_PS + SB_OFF[r]
                    product(ps[:, o:o + P * (SB - r)], k_stack[:, P * r:P * (r + 1)], q_stack[:, P * r:SEQ],
                            start=r < 3)
                for r in range(SB):
                    o = SB_PS + SB_OFF[r]
                    product(ps[:, o:o + P * (SB - r)], qk_hi[hd, 1, P * r:P * (r + 1)], qk_lo[hd, 0, P * r:SEQ])
                last = masked(SB_PS, SB_MASKED, 0)
                last.then_inc(sb_scored, 1)
                fill(0)
                pe.wait_ge(qk_split, pair * 4 + 4)
                pe.wait_ge(fx_w_split, h + FREE)
                pe.wait_ge(sel_ready, h + 1)
                for r in (3, 2, 1, 0):
                    o, width = FX_PS + FX_OFF[r], P * (r + 1)
                    product(ps[:, o:o + width], q_bias_rows[:, e, P * r:P * (r + 1)], k_bias_rows[:, e, 0:width],
                            start=r > 0)
                if last_pair:
                    high_products = [(qk_hi[hd, 2, :], k_bias_rows[hd, e, :]), (qk_hi[hd, 2, :], qk_lo[hd, 2, :])]
                else:
                    pe.wait_ge(stack_in, h * (2 * STACK) + 2 * STACK)
                    high_products = [(q_stack[:], k_stack[:])]
                for q, k in high_products:
                    for r in (3, 2, 1, 0):
                        o, width = FX_PS + FX_OFF[r], P * (r + 1)
                        product(ps[:, o:o + width], q[:, P * r:P * (r + 1)], k[:, 0:width])
                last = masked(FX_PS, FX_MASKED, 1)
                last.then_inc(fx_scored, 1)
                fill(1)
                pe.wait_ge(sb_soft_split, h + 1)
                for part in (sb_hi, sb_lo):
                    for o in range(0, FLAT, 512):
                        end = min(o + 512, FLAT)
                        product(ps[:, SB_PS + o:SB_PS + end], neg_tri[:], part[:, o:end])
                pe.wait_ge(later_split, h + 1)
                for part, soft in ((later_hi, sb_hi), (later_lo, sb_lo)):
                    for r, rhs in ((0, part[:, 0:3 * P]), (1, part[:, LATER_OFF[1]:LATER]),
                                   (2, soft[:, SB_OFF[3]:SB_OFF[3] + P])):
                        o = SB_PS + SB_OFF[r] + P
                        last = product(ps[:, o:o + P * (SB - 1 - r)], neg_one[:], rhs)
                last.then_inc(sb_summed, 1)
                fill(2)
                pe.wait_ge(fx_normed, h * SB + (FREE + 1) * SB)
                for r in range(SB):
                    for c in range(r + 1):
                        o = FX_PS + SB_OFF[c] + P * (r - c)
                        last = nc.tensor.transpose(ps[:, o:o + P], fx_p[:, FX_OFF[r] + P * c:FX_OFF[r] + P * (c + 1)],
                                                   ident[:])
                last.then_inc(fx_turned, 1)
                fill(3)
                pe.wait_ge(v_split, pair * 2 + 2)
                for b, split, ready, hi, lo, mixed in ((0, sb_w_split, h + 1, sb_hi, sb_lo, sb_mixed),
                                                       (1, fx_w_split, h + FREE + 1, fx_hi, fx_lo, fx_mixed)):
                    pe.wait_ge(split, ready)
                    pe.wait_ge(block_read, b0 + (len(order) - 1 + b))
                    for r in range(SB):
                        v = v_parts[:, b, r, e, :, :].rearrange("p t d -> p (t d)")
                        for part in (hi, lo):
                            last = product(ps[:, 512 * (6 + b) + P * r:512 * (7 + b)], v,
                                           part[:, SB_OFF[r]:SB_OFF[r] + P * (SB - r)],
                                           start=r == 0 and part is hi, stop=r == SB - 1 and part is lo)
                    last.then_inc(mixed, 1)

            pe.sem_inc(sb_mixed, FREE)
            pe.sem_inc(fx_mixed, FREE)
            pe.sem_inc(fx_scored, FREE)
            with pe.Fori(0, PAIRS - 1) as pair:
                for e in range(2):
                    half(pair, e, loop_blocks(pair)[e], pair * 8, N_PAIR + 4 * e)
            for e in range(2):
                half(PAIRS - 1, e, LAST_BLOCKS[e], 0, N_LAST + 2 * e)

            with pe.Fori(0, 2) as i:
                for j in range(4):
                    weight_ready(4 * i + (N_MERGE + j))
                    pe.wait_ge(merged, 4 * i + (j + 1))
                    for k in (0, 1, 2, 4, 5, 6, 3, 7):
                        if j == 0 and k % PAIRS == PAIRS - 1:
                            pe.wait_ge(o_split[k // PAIRS], HALVES + FREE)
                        w = (slice(None), (N_MERGE + j) % 4, slice(P * k, P * (k + 1)))
                        last = split_product(bank(MERGE_BANKS[j] + k // PAIRS), w_hi[w], w_lo[w], oT_hi[:, k, :],
                                             oT_lo[:, k, :], k % PAIRS == 0, k % PAIRS == PAIRS - 1)
                    last.then_inc(block_done, 1)

            def turn(s):
                for half_ in range(2):
                    pe.wait_ge(ln_done, 2 * s + half_ + 1)
                    for k in range(4):
                        c = P * (4 * half_ + k)
                        last = nc.tensor.transpose(bank(2 * s + half_)[:, P * k:P * (k + 1)], x1[:, s, c:c + P],
                                                   ident[:])
                    last.then_inc(x1_turned, 1)

            for s in range(SB):
                for half_ in range(2):
                    if s > 0 and half_ == 1:
                        turn(s - 1)
                    for k in range(KB):
                        if s == 0 and half_ == 0:
                            pe.wait_ge(merged, FREE_MERGE + max(k, 4) + 1)
                            pe.wait_ge(wout_split, k + 1)
                        ms = (slice(None), k, slice(P * s, P * (s + 1)))
                        ws = (slice(None), k, slice(512 * half_, 512 * (half_ + 1)))
                        last = split_product(bank(2 * s + half_), mT_hi[ms], mT_lo[ms], wout_hi[ws], wout_lo[ws],
                                             k == 0, k == KB - 1)
                    last.then_inc(out_done, 1)

            def up(n, slot, bank_, start, end):
                weight_ready(n)
                for k in range(KB):
                    w = (slice(None), slot, slice(P * k, P * (k + 1)))
                    last = split_product(bank(bank_)[:, start:end], w_hi[w], w_lo[w], x1T_hi[:, k, start:end],
                                         x1T_lo[:, k, start:end], k == 0 and start == 0, k == KB - 1)
                if end == SEQ:
                    last.then_inc(block_done, 1)

            most = SEQ // 2
            pe.wait_ge(x1_split, SB)
            up(N_UP, N_UP % 4, 0, 0, most)
            up(N_UP + 1, (N_UP + 1) % 4, 1, 0, most)
            turn(SB - 1)
            up(N_UP + 2, (N_UP + 2) % 4, 2, 0, most)
            pe.wait_ge(x1_split, 2 * SB)
            for n in range(N_UP, N_UP + 3):
                up(n, n % 4, n - N_UP, most, SEQ)
            up(N_UP + 3, (N_UP + 3) % 4, 3, 0, SEQ)
            with pe.Fori(1, FB // 2) as i:
                for j in range(2):
                    pe.wait_ge(act_ready, 2 * i + (j + 1))
                    for g in range(2):
                        m = 2 * j + g
                        up(4 * i + (N_UP + m), (N_UP + m) % 4, m, 0, SEQ)

            def down(s, half_, f, slot_a, w_part_hi, w_part_lo, slot_w):
                as_ = (slice(None), slot_a, slice(P * s, P * (s + 1)))
                ws = (slice(None), slot_w, slice(512 * half_, 512 * (half_ + 1)))
                return split_product(bank(DOWN_BANKS[s][half_]), a_hi[as_], a_lo[as_], w_part_hi[ws], w_part_lo[ws],
                                     isinstance(f, int) and f == 0, isinstance(f, int) and f == FB - 1)

            for tokens in ((0, 1), (2, 3)):
                for f in range(2):
                    pe.wait_ge(a_split, f + 1)
                    weight_ready(f + N_DOWN)
                    for s in tokens:
                        if s >= 2:
                            pe.wait_ge(act_ready, FREE_ACT + FB - 3 + s)
                        for half_ in range(2):
                            last = down(s, half_, f, f, w_hi, w_lo, (N_DOWN + f) % 4)
                    if s == SB - 1:
                        last.then_inc(block_done, 1)
            def down_block(f, place):
                pe.wait_ge(a_split, f + 1)
                weight_ready(f + N_DOWN)
                for s in range(SB):
                    for half_ in range(2):
                        last = down(s, half_, f, place, w_hi, w_lo, (N_DOWN + place) % 4)
                last.then_inc(block_done, 1)

            n_loop = (FB - RESIDENT - 2) // 4
            with pe.Fori(0, n_loop) as i:
                for j in range(4):
                    down_block(4 * i + (j + 2), (j + 2) % 4)
            for f in range(2 + 4 * n_loop, FB - RESIDENT):
                down_block(f, f % 4)
            for s in range(SB):
                for half_ in range(2):
                    for f in range(FB - RESIDENT, FB):
                        if s == 0 and half_ == 0:
                            pe.wait_ge(a_split, f + 1)
                            weight_ready(N_DOWN + f)
                        last = down(s, half_, f, a_slot(f), r_hi, r_lo, f - (FB - RESIDENT))
                    last.then_inc(out_done, 1)


V_READ = (0, 6, 7, 1, 2, 3, 4, 5)
MERGE_BANKS = (0, 2, 4, 6)
DOWN_BANKS = ((4, 5), (6, 7), (0, 1), (2, 3))
SET_SIGMOID, SET_LN_EXP, SET_GELU = 2, 6, 10


def loop_blocks(pair):
    gates = {pl: ("gate", pair * 4 + pl, 6 + pl % 2) for pl in range(4)}
    next_qk = {pl: ("qk", pl, 6 + pl % 2) for pl in range(4)}
    return gates, next_qk


LAST_SHARES = (0, 11, 2, 3)
LAST_BLOCKS = [{1: ("gate", NG - 4 + 2 * e, 6), 3: ("gate", NG - 3 + 2 * e, 7)} for e in range(2)]


def kernel(x, w_in, b_in, w_proj_sb, w_proj_fox, w_out, ln1_g, ln1_b, w_up, w_conv, b_conv, w_down, ln2_g, ln2_b):
    import numpy as np
    import concourse.bacc as bacc
    from concourse.bass_utils import run_bass_kernel_spmd

    x2, w_in, b_in = np.asarray(x)[0], np.asarray(w_in)[0], np.asarray(b_in)[0]
    w_out, w_up, w_down = np.asarray(w_out)[0], np.asarray(w_up)[0], np.asarray(w_down)[0]
    w_proj = np.concatenate([np.asarray(w_proj_sb)[0], np.asarray(w_proj_fox)[0]], axis=0)
    w_conv, b_conv = np.asarray(w_conv)[0], np.asarray(b_conv)[0]
    q_sb, k_sb, v_sb, q_fx, k_fx, v_fx, f0, g0 = (0, 512, 1024, 1536, 2048, 2560, 3072, 3072 + N_FORGET)

    def columns(w, start):
        return w[:, start:start + P].reshape(KB, P, P).transpose(1, 0, 2).reshape(P, KB * P)

    head_of = (np.arange(P) // 4) % N_FORGET
    v_cols = np.concatenate([w_in[:, v_sb:v_sb + D_SB], w_in[:, v_fx:v_fx + D_FOX]], axis=1)
    stream = [v_cols[P * k:P * (k + 1)] for k in range(KB)]
    stream.append(columns(w_in[:, f0:f0 + N_FORGET][:, head_of], 0))
    qk = lambda p: [columns(w_in, c + P * p) for c in (q_sb, k_sb, q_fx, k_fx)]
    gate = lambda g: columns(w_in, g0 + P * g)
    stream += qk(0)
    for p in range(PAIRS - 1):
        stream += [gate(4 * p + j) for j in range(4)] + qk(p + 1)
    stream += [gate(g) for g in range(NG - 4, NG)]
    for d in range(KB):
        stream += [columns(w_proj, P * d)]
    for f in range(FB):
        stream += [columns(w_up, P * f), columns(w_up, D_FF + P * f)]
    stream += [w_down[P * f:P * (f + 1)] for f in range(FB)]
    assert len(stream) == N_BLOCKS

    row = np.arange(P)
    sel = np.zeros((P, 6 + N_FORGET), np.float32)
    for c, r, value in ((0, 0, -1), (1, 1, -1), (2, 2, 1), (2, 3, 1), (3, 2, 1), (4, 3, 1), (5, 0, 1), (5, 1, 1)):
        sel[row % 4 == r, c] = value
    for h in range(N_FORGET):
        sel[row % HEAD_DIM // 4 == h, 6 + h] = 1
    vectors = [b_in[c + P * p:c + P * (p + 1)] for p in range(PAIRS) for c in (q_sb, k_sb, q_fx, k_fx)]
    vectors += [b_in[g0 + P * g:g0 + P * (g + 1)] for g in range(NG)]
    vectors += [b_in[f0:f0 + N_FORGET][head_of]]
    vectors += [w_conv[t, P * f:P * (f + 1)] for f in range(FB) for t in range(CONV_WIDTH)]
    vectors += [b_conv[P * f:P * (f + 1)] for f in range(FB)]
    cols = np.concatenate([np.stack(vectors, axis=1), sel], axis=1)
    v_bias = np.concatenate([b_in[v_sb:v_sb + D_SB], b_in[v_fx:v_fx + D_FOX]])
    rows = np.stack([v_bias] + [np.asarray(a)[0] for a in (ln1_g, ln1_b, ln2_g, ln2_b)])
    a, b = np.arange(P)[:, None], np.arange(P)[None, :]
    square = np.stack([a == b, -(a >= b).astype(np.float32), -np.ones((P, P)), -BIG * (a >= b), -BIG * (b > a)],
                      axis=1).astype(np.float32)
    arrays = {"xT_in": x2.T.reshape(KB, P, SEQ), "x_tok_in": x2, "w_stream_in": np.stack(stream),
              "w_out_in": w_out, "cols_in": cols, "rows_in": rows, "square_in": square}
    arrays = {name: np.ascontiguousarray(value) for name, value in arrays.items()}

    nc = bacc.Bacc("TRN2", target_bir_lowering=False, num_devices=1)
    args = [nc.dram_tensor(name, value.shape, mybir.dt.from_np(value.dtype), kind="ExternalInput").ap()
            for name, value in arrays.items()]
    out = nc.dram_tensor("out_dram", (SEQ, D_MODEL), mybir.dt.float32, kind="ExternalOutput").ap()
    layer(nc, *args, out)
    result = run_bass_kernel_spmd(nc, [arrays], core_ids=[0])
    return result.results[0]["out_dram"].reshape(1, SEQ, D_MODEL)
```
